# Optimizing a Trainium2 kernel written in Bass

```python
import jax, jax.numpy as jnp
from jax import lax
import numpy as np

D_MODEL = 1024
BATCH = 1
SEQ = 256
DEPTH = 2

CHUNK = 64
N_MIXERS = 2
EPS = 1e-6
RET_HEADS = 4
RET_QK_DIM = D_MODEL // RET_HEADS
RET_V_DIM = 2 * RET_QK_DIM
RET_QK = RET_HEADS * RET_QK_DIM
RET_V = RET_HEADS * RET_V_DIM
RET_IN = 2 * RET_QK + 2 * RET_V
RET_ROT_BASE = 10000.0
ATT_HEAD_DIM = 64
ATT_Q_HEADS = D_MODEL // ATT_HEAD_DIM
ATT_KV_HEADS = 4
ATT_GROUP = ATT_Q_HEADS // ATT_KV_HEADS
ATT_Q = ATT_Q_HEADS * ATT_HEAD_DIM
ATT_KV = ATT_KV_HEADS * ATT_HEAD_DIM
ATT_IN = ATT_Q + 2 * ATT_KV
WINDOW = 128
WINDOW_CHUNKS = WINDOW // CHUNK
D_FF = 2816
N_RET = (DEPTH + 1) // 2
N_ATT = DEPTH // 2

kernel_name = "hybrid_retention_swa_sink_macaron_trunk"

def rmsnorm(x, g):
    xf = x.astype(jnp.float32)
    y = xf * lax.rsqrt(jnp.mean(xf * xf, axis=-1, keepdims=True) + EPS)
    return (y * g.astype(jnp.float32)).astype(x.dtype)

def swiglu_ffn(x, w_gate_up, w_down):
    a, b = jnp.split(x @ w_gate_up, 2, axis=-1)
    return (jax.nn.silu(a) * b) @ w_down

def rotate_half_pairs(t, cos, sin):
    t1, t2 = jnp.split(t, 2, axis=-1)
    return jnp.concatenate([t1 * cos - t2 * sin, t1 * sin + t2 * cos], axis=-1)

def retention(h, w_in, gn_gain, w_out):
    B, S, _ = h.shape
    dt = h.dtype
    nC = S // CHUNK
    q, k, v, g = jnp.split(h @ w_in, [RET_QK, 2 * RET_QK, 2 * RET_QK + RET_V], axis=-1)
    q = q.reshape(B, S, RET_HEADS, RET_QK_DIM)
    k = k.reshape(B, S, RET_HEADS, RET_QK_DIM)
    v = v.reshape(B, S, RET_HEADS, RET_V_DIM)
    pos = jnp.arange(S, dtype=jnp.float32)
    theta = RET_ROT_BASE ** (-jnp.linspace(0.0, 1.0, RET_QK_DIM // 2, dtype=jnp.float32))
    ang = pos[:, None] * theta[None, :]
    cos = jnp.cos(ang)[:, None, :].astype(dt)
    sin = jnp.sin(ang)[:, None, :].astype(dt)
    q = rotate_half_pairs(q, cos, sin)
    k = rotate_half_pairs(k, cos, sin) * (RET_QK_DIM ** -0.5)

    def to_chunks(t):
        return t.reshape(B, nC, CHUNK, RET_HEADS, t.shape[-1]).transpose(1, 0, 3, 2, 4)

    qc, kc, vc = to_chunks(q), to_chunks(k), to_chunks(v)
    log_gamma = jnp.log(1.0 - 2.0 ** (-5.0 - jnp.arange(RET_HEADS, dtype=jnp.float32)))
    i = jnp.arange(CHUNK, dtype=jnp.float32)
    intra_decay = jnp.exp(log_gamma[:, None, None] * jnp.abs(i[:, None] - i[None, :])).astype(dt)
    query_decay = jnp.exp(log_gamma[:, None] * (i + 1.0))[:, :, None].astype(dt)
    key_decay = jnp.exp(log_gamma[:, None] * (CHUNK - 1.0 - i))[:, :, None].astype(dt)
    chunk_decay = jnp.exp(log_gamma * CHUNK)[:, None, None].astype(dt)

    def step(state, inp):
        q_c, k_c, v_c = inp
        scores = jnp.einsum('bhid,bhjd->bhij', q_c, k_c) * intra_decay
        out = (jnp.einsum('bhij,bhjv->bhiv', scores, v_c)
               + jnp.einsum('bhid,bhdv->bhiv', q_c, state) * query_decay)
        state = state * chunk_decay + jnp.einsum('bhjd,bhjv->bhdv', k_c * key_decay, v_c)
        return state, out

    state0 = jnp.zeros((B, RET_HEADS, RET_QK_DIM, RET_V_DIM), dt)
    _, o = lax.scan(step, state0, (qc, kc, vc))
    o = o.transpose(1, 0, 3, 2, 4).reshape(B, S, RET_HEADS, RET_V_DIM)
    of = o.astype(jnp.float32)
    mu = jnp.mean(of, axis=-1, keepdims=True)
    var = jnp.mean(jnp.square(of - mu), axis=-1, keepdims=True)
    y = ((of - mu) * lax.rsqrt(var + EPS)).reshape(B, S, RET_V) * gn_gain.astype(jnp.float32)
    y = y.astype(dt)
    return (jax.nn.silu(g) * y) @ w_out

def shift_chunks(t, o):
    if o == 0:
        return t
    return jnp.concatenate([jnp.zeros_like(t[:, :o]), t[:, :-o]], axis=1)

def swa_sink_attention(h, w_in, b_in, sinks, w_out, b_out):
    B, S, _ = h.shape
    dt = h.dtype
    nC = S // CHUNK
    q, k, v = jnp.split(h @ w_in + b_in, [ATT_Q, ATT_Q + ATT_KV], axis=-1)
    qb = q.reshape(B, nC, CHUNK, ATT_KV_HEADS, ATT_GROUP, ATT_HEAD_DIM)
    kb = k.reshape(B, nC, CHUNK, ATT_KV_HEADS, ATT_HEAD_DIM)
    vb = v.reshape(B, nC, CHUNK, ATT_KV_HEADS, ATT_HEAD_DIM)
    offsets = list(range(WINDOW_CHUNKS - 1, -1, -1))
    kw = jnp.concatenate([shift_chunks(kb, o) for o in offsets], axis=2)
    vw = jnp.concatenate([shift_chunks(vb, o) for o in offsets], axis=2)
    c_idx = jnp.arange(nC)
    valid = jnp.concatenate([jnp.repeat((c_idx >= o)[:, None], CHUNK, axis=1) for o in offsets], axis=1)
    scores = jnp.einsum('bnqkgd,bnwkd->bnkgqw', qb, kw).astype(jnp.float32) * (ATT_HEAD_DIM ** -0.5)
    scores = jnp.where(valid[None, :, None, None, None, :], scores, -jnp.inf)
    sink = jnp.broadcast_to(sinks.astype(jnp.float32).reshape(1, 1, ATT_KV_HEADS, ATT_GROUP, 1, 1),
                            scores.shape[:-1] + (1,))
    p = jax.nn.softmax(jnp.concatenate([scores, sink], axis=-1), axis=-1)[..., :-1]
    out = jnp.einsum('bnkgqw,bnwkd->bnqkgd', p.astype(dt), vw).reshape(B, S, ATT_Q)
    return out @ w_out + b_out

def setup_inputs(seed: int = 0) -> dict:
    key = jax.random.key(seed)
    ks = jax.random.split(key, 20)
    f32 = jnp.float32

    def w(k, shape, fan_in):
        return jax.random.normal(k, shape, f32) * (fan_in ** -0.5)

    def gain(k, shape):
        return 1.0 + 0.02 * jax.random.normal(k, shape, f32)

    return {
        "x": jax.random.normal(ks[0], (BATCH, SEQ, D_MODEL), f32),
        "ffn1_norm": gain(ks[1], (DEPTH, D_MODEL)),
        "ffn1_w_gate_up": w(ks[2], (DEPTH, D_MODEL, 2 * D_FF), D_MODEL),
        "ffn1_w_down": w(ks[3], (DEPTH, D_FF, D_MODEL), D_FF),
        "mix_norm": gain(ks[4], (DEPTH, D_MODEL)),
        "ret_w_in": w(ks[5], (N_RET, D_MODEL, RET_IN), D_MODEL),
        "ret_gn_gain": gain(ks[6], (N_RET, RET_V)),
        "ret_w_out": w(ks[7], (N_RET, RET_V, D_MODEL), RET_V),
        "att_w_in": w(ks[8], (N_ATT, D_MODEL, ATT_IN), D_MODEL),
        "att_b_in": 0.02 * jax.random.normal(ks[9], (N_ATT, ATT_IN), f32),
        "att_sinks": 0.5 * jax.random.normal(ks[10], (N_ATT, ATT_Q_HEADS), f32),
        "att_w_out": w(ks[11], (N_ATT, ATT_Q, D_MODEL), ATT_Q),
        "att_b_out": 0.02 * jax.random.normal(ks[12], (N_ATT, D_MODEL), f32),
        "ffn2_norm": gain(ks[13], (DEPTH, D_MODEL)),
        "ffn2_w_gate_up": w(ks[14], (DEPTH, D_MODEL, 2 * D_FF), D_MODEL),
        "ffn2_w_down": w(ks[15], (DEPTH, D_FF, D_MODEL), D_FF),
        "final_norm": gain(ks[16], (D_MODEL,)),
    }

def reference(x, ffn1_norm, ffn1_w_gate_up, ffn1_w_down, mix_norm, ret_w_in, ret_gn_gain, ret_w_out,
              att_w_in, att_b_in, att_sinks, att_w_out, att_b_out, ffn2_norm, ffn2_w_gate_up, ffn2_w_down,
              final_norm):
    for i in range(DEPTH):
        x = x + 0.5 * swiglu_ffn(rmsnorm(x, ffn1_norm[i]), ffn1_w_gate_up[i], ffn1_w_down[i])
        hn = rmsnorm(x, mix_norm[i])
        j = i // N_MIXERS
        if i % N_MIXERS == 0:
            mix = retention(hn, ret_w_in[j], ret_gn_gain[j], ret_w_out[j])
        else:
            mix = swa_sink_attention(hn, att_w_in[j], att_b_in[j], att_sinks[j], att_w_out[j], att_b_out[j])
        x = x + mix
        x = x + 0.5 * swiglu_ffn(rmsnorm(x, ffn2_norm[i]), ffn2_w_gate_up[i], ffn2_w_down[i])
    return rmsnorm(x, final_norm)


_drawn_inputs = setup_inputs


def setup_inputs(seed=0):
    import zlib

    import numpy as np

    out = dict(_drawn_inputs(seed))
    spreads = {}
    factors = {'ffn1_norm': 3.971,
     'ret_gn_gain': 17.271,
     'att_b_in': 26.456,
     'att_sinks': 64.0,
     'att_b_out': 28.856,
     'ffn2_norm': 5.599,
     'final_norm': 8.151,
     'att_w_in': 4.535,
     'att_w_out': 4.217}
    for name, (base, spread) in spreads.items():
        noise = np.random.default_rng([zlib.crc32(name.encode()), seed]).standard_normal(out[name].shape)
        drawn = base * np.exp(spread * noise) if base else spread * noise
        out[name] = __import__('jax').numpy.asarray(drawn.astype(out[name].dtype))
    for name, factor in factors.items():
        out[name] = (out[name] * factor).astype(out[name].dtype)
    return out
```

```python
from contextlib import ExitStack

import numpy as np

import concourse.bass as bass
from concourse import mybir

F32 = mybir.dt.float32
F32R = mybir.dt.float32r
ALU = mybir.AluOpType
ACT = mybir.ActivationFunctionType
AXIS_X = mybir.AxisListType.X

P = 128
TOKENS = 256
D_MODEL = 1024
KT = D_MODEL // P
D_FF = 2816
FF_TILES = D_FF // P
FF_PAIRS = FF_TILES // 2
CHUNK = 64
EPS = 1e-6
RET_HEADS = 4
RET_QK = D_MODEL // RET_HEADS
RET_V = 2 * RET_QK
V_TILES = RET_V // P
Q_HEADS, KV_HEADS, HEAD = 16, 4, 64
WORDS = 2048
RING = 3

FFN_CHUNKS = 3 * FF_PAIRS
RET_CHUNKS = 8 * RET_HEADS
ATT_CHUNKS = 10
FFN_AT = [0, FFN_CHUNKS + RET_CHUNKS, 2 * FFN_CHUNKS + RET_CHUNKS, 3 * FFN_CHUNKS + RET_CHUNKS + ATT_CHUNKS]
RET_AT = FFN_CHUNKS
ATT_AT = 3 * FFN_CHUNKS + RET_CHUNKS
CHUNKS = 4 * FFN_CHUNKS + RET_CHUNKS + ATT_CHUNKS
assert CHUNKS % RING == 0 and FFN_CHUNKS % RING == 0
FFN_NORM, RET_NORM, ATT_NORM, LAST_NORM = [0, 2, 3, 5], 1, 4, 6

GAIN = 0
GN_GAIN = GAIN + 7 * KT
BIAS_Q = GN_GAIN + RET_HEADS * V_TILES
BIAS_K = BIAS_Q + 8
BIAS_OUT = BIAS_K + 2
SINKS = BIAS_OUT + KT
BIAS_V = SINKS + 32
PARAMS = BIAS_V + KV_HEADS * HEAD

COS, SIN = 0, TOKENS
IDENT = 2 * TOKENS
DECAY = IDENT + P
BAND = TOKENS + P
CONSTS = DECAY + RET_HEADS * BAND


def trunk(nc, x_in, weights, params_in, consts_in, out):
    with ExitStack() as ctx:
        def sb(name, shape, dt=F32):
            return ctx.enter_context(nc.sbuf_tensor(name, shape, dt))

        def sem(name):
            return ctx.enter_context(nc.semaphore(name))

        raw = sb("raw", [P, RING, WORDS])
        w_hi = sb("w_hi", [P, RING, WORDS], F32R)
        w_lo = sb("w_lo", [P, RING, WORDS], F32R)
        params = sb("params", [P, PARAMS])
        consts = sb("consts", [P, CONSTS])
        ones = sb("ones", [P, P])
        eps = sb("eps", [P, 1])
        x = sb("x", [P, KT, TOKENS])
        a_hi = sb("a_hi", [P, KT, TOKENS], F32R)
        a_lo = sb("a_lo", [P, KT, TOKENS], F32R)
        sq_sum = sb("sq_sum", [P, 2, TOKENS])
        mean_sq = sb("mean_sq", [P, TOKENS + 2])
        root = sb("root", [P, TOKENS + 2])
        guess = sb("guess", [P, TOKENS + 2])
        newton = sb("newton", [P, TOKENS + 2])
        rstd = sb("rstd", [P, TOKENS + 2])
        gate_up = sb("gate_up", [P, 2, 2, TOKENS])
        gate_act = sb("gate_act", [P, 2, TOKENS])
        h = sb("h", [P, 2, TOKENS])
        h_hi = sb("h_hi", [P, 2, 2, TOKENS], F32R)
        h_lo = sb("h_lo", [P, 2, 2, TOKENS], F32R)
        cos_r = sb("cos_r", [P, 2, TOKENS])
        rope_a = sb("rope_a", [P, 2, TOKENS])
        rope_b = sb("rope_b", [P, 2, TOKENS])
        qk = sb("qk", [P, 2, 2, 2, TOKENS])
        decayed = sb("decayed", [P, RET_HEADS, BAND])
        values = sb("values", [P, 2, RET_HEADS * RET_V])
        o_head = sb("o_head", [P, V_TILES, TOKENS])
        o_sq = sb("o_sq", [P, V_TILES, TOKENS])
        o_sum = sb("o_sum", [P, 2, TOKENS])
        g_act = sb("g_act", [P, 2, V_TILES, TOKENS])
        x_sq = [buf[:, 2 * n:2 * n + 2, :] for buf in (o_head, o_sq) for n in range(2)]
        y_hi = sb("y_hi", [P, 8, TOKENS], F32R)
        y_lo = sb("y_lo", [P, 8, TOKENS], F32R)
        att_k = rope_a
        att_v = g_act[:, 1, 0:3, :]
        att_q = qk[:, :, :, :, :].rearrange("p a b c t -> p (a b c) t")
        probs_t = values[:, :, :].rearrange("p a (i n) -> p (a i) n", n=4 * P)
        exps = [half.rearrange("p c (d t) -> p (c d) t", d=2)
                for buf in (g_act[:, 0, :, :], o_head, o_sq) for half in (buf[:, 0:2, :], buf[:, 2:4, :])]
        row_max = sb("row_max", [P, 4])
        neg_max = sb("neg_max", [P, 2, 4])
        neg_sinks = sb("neg_sinks", [P, 32])
        sink_arg = sb("sink_arg", [P, 2, 4])
        sink_exp = sb("sink_exp", [P, 2, 4])
        exp_sum = sb("exp_sum", [P, 2, 4])
        denom = sb("denom", [P, 4])
        inv_denom = sb("inv_denom", [P, 4])
        result = o_head
        result2 = o_sq

        banks = [ctx.enter_context(nc.psum_tensor(f"bank{i}", [P, 2, TOKENS], F32)) for i in range(8)]
        acc = banks[0:4]
        proj = banks[4:6]
        misc = banks[6:8]

        x_landed = [sem(f"x_landed{p}") for p in range(4)]
        first_landed = [sem(f"first_landed{q}") for q in range(4)]
        consts_landed = sem("consts_landed")
        first_rounded = sem("first_rounded")
        first_split = sem("first_split")
        params_landed = sem("params_landed")
        raw_landed = [sem(f"raw_landed{s}") for s in range(RING)]
        ones_set = sem("ones_set")
        hi_done = sem("hi_done")
        split_done = sem("split_done")
        chunk_used = sem("chunk_used")
        acc_ready = sem("acc_ready")
        x_new = sem("x_new")
        a_hi_done = sem("a_hi_done")
        a_split = sem("a_split")
        sq_done = sem("sq_done")
        sum_done = sem("sum_done")
        stats_ready = sem("stats_ready")
        root_done = sem("root_done")
        norm_step = sem("norm_step")
        scaled = sem("scaled")
        gated = sem("gated")
        h_done = sem("h_done")
        h_hi_done = sem("h_hi_done")
        h_split = sem("h_split")
        tables_ready = sem("tables_ready")
        roped = sem("roped")
        rope_sum = sem("rope_sum")
        scores_ready = sem("scores_ready")
        decay_done = sem("decay_done")
        v_kept = sem("v_kept")
        o_ready = sem("o_ready")
        o_kept = sem("o_kept")
        o_added = sem("o_added")
        mean_ready = sem("mean_ready")
        centred = sem("centred")
        centred_scaled = sem("centred_scaled")
        sinks_ready = sem("sinks_ready")
        o_squared = sem("o_squared")
        var_ready = sem("var_ready")
        var_root = sem("var_root")
        gn_step = sem("gn_step")
        g_scaled = sem("g_scaled")
        g_done = sem("g_done")
        y_done = sem("y_done")
        y_hi_done = sem("y_hi_done")
        y_split = sem("y_split")
        kqv_scaled = sem("kqv_scaled")
        k_done = sem("k_done")
        v_done = sem("v_done")
        v_shifted = sem("v_shifted")
        q_done = sem("q_done")
        att_scores = sem("att_scores")
        masked = sem("masked")
        max_step = sem("max_step")
        exp_done = sem("exp_done")
        soft_step = sem("soft_step")
        probs_done = sem("probs_done")
        turned = sem("turned")
        turned_kept = sem("turned_kept")
        mixed = sem("mixed")
        mixed_hi = sem("mixed_hi")
        mixed_split = sem("mixed_split")
        result_done = sem("result_done")
        stored = sem("stored")

        def scores_bank(u):
            return (misc, acc[2:4], misc, proj)[u // 2][u % 2]

        def turned_bank(u):
            return (acc, acc, misc, proj)[u // 2][u % 2]

        def mix_bank(g, qt):
            bank = (acc[2:4] if g == 0 else misc)[qt]
            return bank[:, :, :].rearrange("p a (b t) -> p (a b) t", t=P)

        def used(c):
            return c + 1

        def gate_chunk(f, j):
            return FFN_AT[f] + (j if j < 2 else 2 + 3 * (j // 2 - 1) + j % 2)

        def down_chunk(f, i):
            return FFN_AT[f] + (4 + 3 * i if i < FF_PAIRS - 1 else FFN_CHUNKS - 1)

        def gain(e, k):
            return params[:, GAIN + e * KT + k:GAIN + e * KT + k + 1]

        def row_rstd():
            return rstd[:, 0:TOKENS].unsqueeze(1).to_broadcast([P, 2, TOKENS])

        def q_chunk(hd):
            return RET_AT + 2 * hd

        def k_chunk(hd):
            return RET_AT + 2 * hd + 1

        def v_chunk(hd, half):
            return RET_AT + 2 * RET_HEADS + 2 * hd + half

        RET_TAIL = [("g", 0), ("g", 1), ("o", 0), ("g", 2), ("o", 1), ("g", 3), ("o", 2), ("o", 3)]

        def tail_chunk(kind, hd, half):
            return RET_AT + 4 * RET_HEADS + 2 * RET_TAIL.index((kind, hd)) + half

        def quarter(q):
            return slice(q * WORDS // 4, (q + 1) * WORDS // 4)

        block = ctx.enter_context(nc.Block())

        @block.sync
        def _(sp):
            sp.dma_start(params[:, :], params_in).then_inc(params_landed, 16)
            for p in range(4):
                sp.dma_start(x[:, 2 * p:2 * p + 2, :], x_in[:, 2 * p:2 * p + 2, :]).then_inc(x_landed[p], 16)
            for s in range(1, RING):
                sp.dma_start(raw[:, s, :], weights[s]).then_inc(raw_landed[s], 16)
            sp.dma_start(consts[:, :], consts_in).then_inc(consts_landed, 16)
            with sp.Fori(1, CHUNKS // RING) as turn:
                for s in range(RING):
                    sp.wait_ge(split_done, turn * RING + max(s - RING, 1 - RING))
                    sp.dma_start(raw[:, s, :], weights[bass.ds(turn * RING + s, 1)].rearrange("o p w -> (o p) w"))\
                      .then_inc(raw_landed[s], 16)
            for half in range(2):
                sp.wait_ge(result_done, 4 * (half + 1))
                sp.dma_start(out[:, 4 * half:4 * half + 4, :], (result, result2)[half][:, :, :]).then_inc(stored, 16)
            sp.wait_ge(stored, 32)

        @block.gpsimd
        def _(pool):
            nc.gpsimd.memset(ones[:, :], 1.0).then_inc(ones_set, 1)
            nc.gpsimd.memset(eps[:, :], EPS).then_inc(ones_set, 1)
            for e in range(7):
                if e:
                    pool.wait_ge(stats_ready, e)
                for p in range(1, 4):
                    pool.wait_ge(sq_done, 4 * e + p + 1)
                    if p > 1:
                        pool.wait_ge(sum_done, 3 * e + p - 1)
                    first = x_sq[0] if p == 1 else sq_sum[:, :, :]
                    nc.gpsimd.tensor_tensor(sq_sum[:, :, :], first, x_sq[p], ALU.add).then_inc(sum_done, 1)

        @block.scalar
        def _(act):
            def round_chunk(c, turn=0):
                s = c % RING
                act.wait_ge(raw_landed[s], 16 * turn + 16 * (c // RING + (1 if s else 0)))
                if c >= RING:
                    act.wait_ge(chunk_used, RING * turn + used(c - RING))
                nc.scalar.activation(w_hi[:, s, :], raw[:, s, :], ACT.Copy).then_inc(hi_done, 1)

            def round_after(c, turn=0):
                if c + RING < CHUNKS:
                    round_chunk(c + RING, turn)

            def norm_input(e):
                def square(p):
                    if e and p == 0:
                        act.wait_ge(sum_done, 3 * e)
                    nc.scalar.activation(x_sq[p], x[:, 2 * p:2 * p + 2, :], ACT.Square).then_inc(sq_done, 1)

                for p in range(4):
                    if e:
                        act.wait_ge(x_new, 4 * (e - 1) + p + 1)
                    else:
                        act.wait_ge(first_landed[p], 16)
                        nc.scalar.activation(w_hi[:, 0, quarter(p)], raw[:, 0, quarter(p)], ACT.Copy)\
                          .then_inc(first_rounded, 1)
                        act.wait_ge(x_landed[p], 16)
                    if e < LAST_NORM:
                        for k in (2 * p, 2 * p + 1):
                            nc.scalar.activation(a_hi[:, k, :], x[:, k, :], ACT.Copy, scale=gain(e, k))\
                              .then_inc(a_hi_done, 1)
                    if e:
                        square(p)
                if e == 0:
                    for c in range(1, RING):
                        round_chunk(c)
                    for p in range(4):
                        square(p)

            def norm_root(e):
                act.wait_ge(stats_ready, e + 1)
                if e:
                    act.wait_ge(norm_step, 6 * e)
                n = TOKENS + 2 if e in (RET_NORM, ATT_NORM) else TOKENS
                nc.scalar.activation(root[:, 0:n], misc[1][:, :, :].rearrange("p a t -> p (a t)")[:, 0:n],
                                     ACT.Sqrt, scale=1.0 / D_MODEL, bias=eps[:, :]).then_inc(root_done, 1)

            def gate_tile(f, jt, i=0):
                t = f * FF_TILES + jt
                act.wait_ge(scaled, 2 * i + t + 1)
                if t >= 2:
                    act.wait_ge(h_done, 2 * i + t - 1)
                nc.scalar.activation(gate_act[:, jt % 2, :], gate_up[:, jt % 2, 0, :], ACT.Silu).then_inc(gated, 1)

            def round_h(f, pair, buf, i=0):
                t = f * FF_PAIRS + pair
                act.wait_ge(h_done, 2 * i + 2 * t + 2)
                nc.scalar.activation(h_hi[:, buf], h[:, :, :], ACT.Copy).then_inc(h_hi_done, 1)

            def ffn(f):
                n0 = FFN_AT[f]
                norm_input(FFN_NORM[f])
                if n0:
                    round_after(n0 - 2)
                    round_after(n0 - 1)
                norm_root(FFN_NORM[f])
                for j in range(2):
                    round_after(n0 + j)
                    gate_tile(f, j)
                round_h(f, 0, 0)
                with act.Fori(0, FF_PAIRS - 2) as i:
                    for j in (2, 3):
                        round_after(gate_chunk(f, j), i)
                        gate_tile(f, j, i)
                    act.wait_ge(chunk_used, RING * i + used(down_chunk(f, 0)))
                    round_h(f, 1, 0, i)
                    round_after(down_chunk(f, 0), i)
                last = FF_TILES - 2
                round_after(gate_chunk(f, last))
                gate_tile(f, last)
                gate_tile(f, last + 1)
                round_h(f, FF_PAIRS - 1, 1)
                round_after(gate_chunk(f, last + 1))

            def retention():
                norm_input(RET_NORM)
                round_after(RET_AT - 2)
                round_after(RET_AT - 1)
                norm_root(RET_NORM)
                for c in range(q_chunk(0), v_chunk(0, 0)):
                    round_after(c)
                for hd in range(RET_HEADS):
                    round_after(v_chunk(hd, 0))
                    act.wait_ge(chunk_used, used(v_chunk(hd, 1)))
                    act.wait_ge(norm_step, 6 * (RET_NORM + 1))
                    for tt in range(2):
                        nc.scalar.activation(values[:, tt, hd * RET_V:(hd + 1) * RET_V],
                                             acc[2 * (hd % 2) + tt][:, :, :].rearrange("p a t -> p (a t)"), ACT.Copy,
                                             scale=rstd[:, TOKENS + tt:TOKENS + tt + 1]).then_inc(v_kept, 1)
                    round_after(v_chunk(hd, 1))
                for kind, hd in RET_TAIL:
                    if kind == "g":
                        act.wait_ge(o_ready, hd + 1)
                        if hd:
                            act.wait_ge(y_done, 4 * hd)
                        for half in range(2):
                            nc.scalar.activation(o_head[:, 2 * half:2 * half + 2, :], misc[half][:, :, :], ACT.Copy)\
                              .then_inc(o_kept, 1)
                    for half in range(2):
                        if tail_chunk(kind, hd, half) < RET_AT + RET_CHUNKS - 2:
                            round_after(tail_chunk(kind, hd, half))
                        if kind == "g":
                            act.wait_ge(g_scaled, 2 * hd + half + 1)
                            nc.scalar.activation(g_act[:, hd % 2, 2 * half:2 * half + 2, :],
                                                 gate_up[:, half], ACT.Silu).then_inc(g_done, 1)
                            if half == 0:
                                act.wait_ge(centred, hd + 1)
                                if hd:
                                    act.wait_ge(o_added, 2 * hd)
                                nc.scalar.activation(o_sq[:, :, :], o_head[:, :, :], ACT.Square)\
                                  .then_inc(o_squared, 1)
                            else:
                                act.wait_ge(var_ready, hd + 1)
                                act.wait_ge(gn_step, 6 * hd)
                                nc.scalar.activation(root[:, 0:TOKENS], misc[1][:, 0, :], ACT.Sqrt,
                                                     scale=1.0 / RET_V, bias=eps[:, :]).then_inc(var_root, 1)
                                act.wait_ge(y_done, 4 * hd + 4)
                                if hd >= 2:
                                    act.wait_ge(chunk_used, used(tail_chunk("o", hd - 2, 1)))
                                nc.scalar.activation(y_hi[:, 4 * (hd % 2):4 * (hd % 2) + 4, :], o_sq[:, :, :],
                                                     ACT.Copy).then_inc(y_hi_done, 1)

            def attention():
                n0 = ATT_AT
                norm_input(ATT_NORM)
                round_after(n0 - 2)
                round_after(n0 - 1)
                norm_root(ATT_NORM)
                round_after(n0)
                for t in range(2):
                    act.wait_ge(kqv_scaled, 1)
                    nc.scalar.activation(att_k[:, t, :], gate_up[:, 0, t, :], ACT.Identity,
                                         bias=params[:, BIAS_K + t:BIAS_K + t + 1]).then_inc(k_done, 1)
                round_after(n0 + 1)
                act.wait_ge(v_done, 2)
                act.dma_start(att_v[0:64, 2, :], att_v[64:128, 0, :]).then_inc(v_shifted, 16)
                act.dma_start(att_v[64:128, 2, :], att_v[0:64, 1, :]).then_inc(v_shifted, 16)

                def q_tiles(c):
                    if c < 3:
                        round_after(n0 + 2 + c)
                    act.wait_ge(kqv_scaled, 2 + c)
                    for t in range(2):
                        q = 2 * c + t
                        nc.scalar.activation(att_q[:, q, :], gate_up[:, (c + 1) % 2, t, :], ACT.Identity,
                                             bias=params[:, BIAS_Q + q:BIAS_Q + q + 1]).then_inc(q_done, 1)

                def exp_tile(i):
                    act.wait_ge(max_step, 3 * i + 3)
                    if i >= 6:
                        act.wait_ge(turned, i - 5)
                    if i >= 2:
                        act.wait_ge(soft_step, 2 * i - 3)
                    for b in range(4):
                        nc.scalar.activation(exps[i % 6][:, b, :], scores_bank(i)[:, b // 2, (b % 2) * P:(b % 2 + 1) * P],
                                             ACT.Exp, scale=HEAD ** -0.5, bias=neg_max[:, i % 2, b:b + 1],
                                             accum_out=exp_sum[:, i % 2, b:b + 1]).then_inc(exp_done, 1)
                    nc.scalar.activation(sink_exp[:, i % 2, :], sink_arg[:, i % 2, :], ACT.Exp).then_inc(exp_done, 1)

                def keep_turned(i):
                    act.wait_ge(turned, i + 1)
                    c, f = i // 2, i % 2
                    nc.scalar.activation(probs_t[:, 2 * c:2 * c + 2, 2 * f * P:(2 * f + 2) * P],
                                         turned_bank(i)[:, :, :], ACT.Copy).then_inc(turned_kept, 1)

                def round_mixed(g):
                    act.wait_ge(mixed, g + 1)
                    for qt in range(2):
                        nc.scalar.activation(y_hi[:, 4 * g:4 * g + 4, qt * P:(qt + 1) * P],
                                             mix_bank(g, qt), ACT.Copy).then_inc(mixed_hi, 1)

                q_tiles(0)
                q_tiles(1)
                exp_tile(0)
                exp_tile(1)
                q_tiles(2)
                exp_tile(2)
                exp_tile(3)
                keep_turned(0)
                keep_turned(1)
                q_tiles(3)
                keep_turned(2)
                keep_turned(3)
                exp_tile(4)
                round_mixed(0)
                exp_tile(5)
                exp_tile(6)
                exp_tile(7)
                round_after(n0 + 5)
                for u in range(4, 8):
                    keep_turned(u)
                round_mixed(1)
                round_after(n0 + 6)
                round_after(n0 + 7)

            for q in range(4):
                act.dma_start(raw[:, 0, quarter(q)], weights[0, :, quarter(q)]).then_inc(first_landed[q], 16)
            act.wait_ge(params_landed, 16)
            act.wait_ge(ones_set, 2)
            ffn(0)
            retention()
            ffn(1)
            ffn(2)
            attention()
            ffn(3)
            norm_input(LAST_NORM)
            norm_root(LAST_NORM)

        @block.vector
        def _(dve):
            def split_chunk(c, turn=0):
                s = c % RING
                dve.wait_ge(hi_done, RING * turn + c)
                nc.vector.tensor_tensor(w_lo[:, s, :], raw[:, s, :], w_hi[:, s, :].bitcast(F32), ALU.subtract)\
                  .then_inc(split_done, 1)

            def split_after(c, turn=0):
                if c + RING < CHUNKS:
                    split_chunk(c + RING, turn)

            def pair_ready(e, p, last_chunk):
                if p < 3:
                    dve.wait_ge(acc_ready, 3 * (e - 1) + p + 1)
                else:
                    dve.wait_ge(chunk_used, used(last_chunk))

            def residual(e, p, last_chunk):
                pair_ready(e, p, last_chunk)
                two = slice(2 * p, 2 * p + 2)
                if e == ATT_NORM + 1:
                    for d in (2 * p, 2 * p + 1):
                        last = nc.vector.scalar_tensor_tensor(x[:, d, :], acc[p][:, d % 2, :],
                                                              params[:, BIAS_OUT + d:BIAS_OUT + d + 1], x[:, d, :],
                                                              ALU.add, ALU.add)
                    last.then_inc(x_new, 1)
                else:
                    factor = 1.0 if e == RET_NORM + 1 else 0.5
                    nc.vector.scalar_tensor_tensor(x[:, two, :], acc[p][:, :, :], factor, x[:, two, :],
                                                   ALU.mult, ALU.add).then_inc(x_new, 1)

            def norm_input(e, last_chunk):
                for p in range(4):
                    if e:
                        residual(e, p, last_chunk)
                    if e < LAST_NORM:
                        if e == 0:
                            dve.wait_ge(first_rounded, p + 1)
                            nc.vector.tensor_tensor(w_lo[:, 0, quarter(p)], raw[:, 0, quarter(p)],
                                                    w_hi[:, 0, quarter(p)].bitcast(F32), ALU.subtract)\
                              .then_inc(first_split, 1)
                        for k in (2 * p, 2 * p + 1):
                            dve.wait_ge(a_hi_done, 8 * e + k + 1)
                            nc.vector.scalar_tensor_tensor(a_lo[:, k, :], x[:, k, :], gain(e, k),
                                                           a_hi[:, k, :].bitcast(F32), ALU.mult, ALU.subtract)\
                              .then_inc(a_split, 1)
                if e == 0:
                    for c in range(1, RING):
                        split_chunk(c)

            def inverse_root(e, n, psum, scale, ready, count, rooted, rooted_count, step, base, target):
                dve.wait_ge(ready, count)
                nc.vector.tensor_scalar(mean_sq[:, 0:n], psum, scale, EPS, ALU.mult, ALU.add).then_inc(step, 1)
                dve.wait_ge(rooted, rooted_count)
                nc.vector.reciprocal(guess[:, 0:n], root[:, 0:n]).then_inc(step, 1)
                dve.wait_ge(step, base + 2)
                nc.vector.tensor_tensor(newton[:, 0:n], guess[:, 0:n], guess[:, 0:n], ALU.mult).then_inc(step, 1)
                dve.wait_ge(step, base + 3)
                nc.vector.tensor_tensor(newton[:, 0:n], newton[:, 0:n], mean_sq[:, 0:n], ALU.mult).then_inc(step, 1)
                dve.wait_ge(step, base + 4)
                nc.vector.tensor_scalar(newton[:, 0:n], newton[:, 0:n], -0.5, 1.5, ALU.mult, ALU.add).then_inc(step, 1)
                dve.wait_ge(step, base + 5)
                nc.vector.tensor_tensor(target[:, 0:n], guess[:, 0:n], newton[:, 0:n], ALU.mult).then_inc(step, 1)

            def norm_rstd(e):
                n = TOKENS + 2 if e in (RET_NORM, ATT_NORM) else TOKENS
                dve.wait_ge(root_done, e + 1)
                inverse_root(e, n, misc[1][:, :, :].rearrange("p a t -> p (a t)")[:, 0:n], 1.0 / D_MODEL,
                             stats_ready, e + 1, root_done, e + 1, norm_step, 6 * e, rstd)
                dve.wait_ge(norm_step, 6 * e + 6)

            def scale_tile(f, jt, i=0):
                t = f * FF_TILES + jt
                dve.wait_ge(chunk_used, RING * i + used(gate_chunk(f, jt)))
                if t >= 2:
                    dve.wait_ge(h_done, 2 * i + t - 1)
                    dve.wait_ge(gated, 2 * i + t - 1)
                nc.vector.tensor_tensor(gate_up[:, jt % 2], proj[jt % 2][:, :, :], row_rstd(), ALU.mult)\
                  .then_inc(scaled, 1)

            def h_tile(f, jt, i=0):
                t = f * FF_TILES + jt
                dve.wait_ge(gated, 2 * i + t + 1)
                if t >= 2:
                    dve.wait_ge(h_split, i + (t // 2))
                nc.vector.tensor_tensor(h[:, jt % 2, :], gate_act[:, jt % 2, :], gate_up[:, jt % 2, 1, :], ALU.mult)\
                  .then_inc(h_done, 1)

            def split_h(f, pair, buf, i=0):
                t = f * FF_PAIRS + pair
                dve.wait_ge(h_hi_done, i + t + 1)
                dve.wait_ge(h_done, 2 * i + 2 * t + 2)
                nc.vector.tensor_tensor(h_lo[:, buf], h[:, :, :], h_hi[:, buf].bitcast(F32), ALU.subtract)\
                  .then_inc(h_split, 1)

            def ffn(f):
                n0 = FFN_AT[f]
                norm_input(FFN_NORM[f], n0 - 1)
                if n0:
                    split_after(n0 - 2)
                    split_after(n0 - 1)
                norm_rstd(FFN_NORM[f])
                for j in range(2):
                    scale_tile(f, j)
                    split_after(n0 + j)
                    h_tile(f, j)
                split_h(f, 0, 0)
                with dve.Fori(0, FF_PAIRS - 2) as i:
                    for j in (2, 3):
                        scale_tile(f, j, i)
                        split_after(gate_chunk(f, j), i)
                        h_tile(f, j, i)
                    split_h(f, 1, 0, i)
                    split_after(down_chunk(f, 0), i)
                last = FF_TILES - 2
                scale_tile(f, last)
                split_after(gate_chunk(f, last))
                h_tile(f, last)
                scale_tile(f, last + 1)
                h_tile(f, last + 1)
                split_h(f, FF_PAIRS - 1, 1)
                split_after(gate_chunk(f, last + 1))

            def rope(hd, which):
                c = (q_chunk, k_chunk)[which](hd)
                done = 2 * hd + which
                dve.wait_ge(chunk_used, used(c))
                if done:
                    dve.wait_ge(rope_sum, 2 * done)
                two = [cos_r[:, t, :].unsqueeze(1).to_broadcast([P, 2, TOKENS]) for t in range(2)]
                nc.vector.tensor_tensor(rope_a[:, :, :], proj[which][:, :, :], two[0], ALU.mult).then_inc(roped, 1)
                nc.vector.tensor_tensor(rope_b[:, :, :], proj[which][:, :, :], two[1], ALU.mult).then_inc(roped, 1)
                dve.wait_ge(roped, 2 * done + 2)
                if hd >= 2:
                    dve.wait_ge(scores_ready, hd - 1)
                nc.vector.tensor_tensor(qk[:, hd % 2, which, 0, :], rope_a[:, 0, :], rope_b[:, 1, :], ALU.subtract)\
                  .then_inc(rope_sum, 1)
                nc.vector.tensor_tensor(qk[:, hd % 2, which, 1, :], rope_b[:, 0, :], rope_a[:, 1, :], ALU.add)\
                  .then_inc(rope_sum, 1)

            def decay(hd):
                dve.wait_ge(scores_ready, hd + 1)
                nc.vector.tensor_tensor(decayed[:, hd, :], misc[hd % 2][:, :, :].rearrange("p a t -> p (a t)")[:, 0:BAND],
                                        consts[:, DECAY + hd * BAND:DECAY + (hd + 1) * BAND], ALU.mult)\
                  .then_inc(decay_done, 1)

            def group_norm(hd):
                base = 6 * hd
                dve.wait_ge(var_root, hd + 1)
                inverse_root(0, TOKENS, misc[1][:, 0, :], 1.0 / RET_V, var_ready, hd + 1, var_root, hd + 1,
                             gn_step, base, mean_sq)
                dve.wait_ge(gn_step, base + 6)
                wide = mean_sq[:, 0:TOKENS].unsqueeze(1).to_broadcast([P, V_TILES, TOKENS])
                nc.vector.tensor_tensor(o_head[:, :, :], o_head[:, :, :], wide, ALU.mult).then_inc(centred_scaled, 1)
                dve.wait_ge(centred_scaled, hd + 1)
                dve.wait_ge(g_done, 2 * hd + 2)
                for t in range(V_TILES):
                    n = GN_GAIN + hd * V_TILES + t
                    nc.vector.scalar_tensor_tensor(o_sq[:, t, :], o_head[:, t, :], params[:, n:n + 1],
                                                   g_act[:, hd % 2, t, :], ALU.mult, ALU.mult).then_inc(y_done, 1)
                dve.wait_ge(y_hi_done, hd + 1)
                half = slice(4 * (hd % 2), 4 * (hd % 2) + 4)
                nc.vector.tensor_tensor(y_lo[:, half, :], o_sq[:, :, :], y_hi[:, half, :].bitcast(F32), ALU.subtract)\
                  .then_inc(y_split, 1)

            def retention():
                norm_input(RET_NORM, RET_AT - 1)
                split_after(RET_AT - 2)
                split_after(RET_AT - 1)
                norm_rstd(RET_NORM)
                dve.wait_ge(consts_landed, 16)
                for t in range(2):
                    nc.vector.tensor_tensor(cos_r[:, t, :], consts[:, COS + t * TOKENS:COS + (t + 1) * TOKENS],
                                            rstd[:, 0:TOKENS], ALU.mult).then_inc(tables_ready, 1)
                dve.wait_ge(tables_ready, 2)
                for hd in range(RET_HEADS):
                    for which in range(2):
                        rope(hd, which)
                        if hd and which == 0:
                            decay(hd - 1)
                        split_after((q_chunk, k_chunk)[which](hd))
                for hd in range(RET_HEADS):
                    split_after(v_chunk(hd, 0))
                    if hd == 0:
                        decay(RET_HEADS - 1)
                    split_after(v_chunk(hd, 1))
                for kind, hd in RET_TAIL:
                    for half in range(2):
                        c = tail_chunk(kind, hd, half)
                        if kind == "g":
                            if half == 0:
                                dve.wait_ge(o_kept, 2 * hd + 2)
                                nc.vector.tensor_tensor(o_sum[:, :, :], o_head[:, 0:2, :], o_head[:, 2:4, :], ALU.add)\
                                  .then_inc(o_added, 1)
                            dve.wait_ge(chunk_used, used(c))
                            dve.wait_ge(h_done, FF_TILES)
                            if hd:
                                dve.wait_ge(g_done, 2 * hd + half - 1)
                            nc.vector.tensor_tensor(gate_up[:, half], proj[half][:, :, :], row_rstd(), ALU.mult)\
                              .then_inc(g_scaled, 1)
                            if half == 0:
                                dve.wait_ge(mean_ready, hd + 1)
                                mean = misc[0][:, 0, :].unsqueeze(1).to_broadcast([P, V_TILES, TOKENS])
                                nc.vector.scalar_tensor_tensor(o_head[:, :, :], mean, -1.0 / RET_V, o_head[:, :, :],
                                                               ALU.mult, ALU.add).then_inc(centred, 1)
                            split_after(c)
                            if half == 0:
                                dve.wait_ge(o_squared, hd + 1)
                                nc.vector.tensor_tensor(o_sum[:, :, :], o_sq[:, 0:2, :], o_sq[:, 2:4, :], ALU.add)\
                                  .then_inc(o_added, 1)
                            else:
                                group_norm(hd)
                        elif c < RET_AT + RET_CHUNKS - 2:
                            split_after(c)

            def attention():
                n0 = ATT_AT
                norm_input(ATT_NORM, n0 - 1)
                split_after(n0 - 2)
                split_after(n0 - 1)
                norm_rstd(ATT_NORM)
                nc.vector.tensor_scalar(neg_sinks[:, :], params[:, SINKS:SINKS + 32], -1.0, None, ALU.mult)\
                  .then_inc(sinks_ready, 1)
                dve.wait_ge(sinks_ready, 1)
                dve.wait_ge(chunk_used, used(n0))
                nc.vector.tensor_tensor(gate_up[:, 0], proj[0][:, :, :], row_rstd(), ALU.mult).then_inc(kqv_scaled, 1)
                split_after(n0)
                dve.wait_ge(chunk_used, used(n0 + 1))
                for tt in range(2):
                    nc.vector.scalar_tensor_tensor(att_v[:, tt, :], proj[1][:, tt, :],
                                                   rstd[:, TOKENS + tt:TOKENS + tt + 1],
                                                   params[:, BIAS_V:BIAS_V + KV_HEADS * HEAD], ALU.mult, ALU.add)\
                      .then_inc(v_done, 1)
                split_after(n0 + 1)

                def q_tiles(c):
                    dve.wait_ge(chunk_used, used(n0 + 2 + c))
                    if c == 1:
                        dve.wait_ge(k_done, 2)
                    if c >= 2:
                        dve.wait_ge(q_done, 2 * (c - 1))
                    nc.vector.tensor_tensor(gate_up[:, (c + 1) % 2], proj[c % 2][:, :, :], row_rstd(), ALU.mult)\
                      .then_inc(kqv_scaled, 1)
                    if c < 3:
                        split_after(n0 + 2 + c)

                def maxima(i):
                    dve.wait_ge(att_scores, i + 1)
                    bank = scores_bank(i)[:, :, :].rearrange("p a t -> p (a t)")
                    nc.vector.memset(scores_bank(i)[0:64, :, 64:128], -3.0e38).then_inc(masked, 1)
                    dve.wait_ge(masked, i + 1)
                    nc.vector.tensor_reduce(row_max[:, :], bank.rearrange("p (b t) -> p b t", t=P), AXIS_X, ALU.max)\
                      .then_inc(max_step, 1)
                    dve.wait_ge(max_step, 3 * i + 1)
                    if i >= 2:
                        dve.wait_ge(exp_done, 5 * (i - 1))
                    sinks = neg_sinks[:, 4 * i:4 * i + 4]
                    nc.vector.scalar_tensor_tensor(neg_max[:, i % 2, :], row_max[:, :], -HEAD ** -0.5, sinks,
                                                   ALU.mult, ALU.min).then_inc(max_step, 1)
                    dve.wait_ge(max_step, 3 * i + 2)
                    nc.vector.tensor_tensor(sink_arg[:, i % 2, :], neg_max[:, i % 2, :], sinks, ALU.subtract)\
                      .then_inc(max_step, 1)

                def normalise(i):
                    dve.wait_ge(exp_done, 5 * i + 5)
                    nc.vector.tensor_tensor(denom[:, :], exp_sum[:, i % 2, :], sink_exp[:, i % 2, :], ALU.add)\
                      .then_inc(soft_step, 1)
                    dve.wait_ge(soft_step, 2 * i + 1)
                    nc.vector.reciprocal(inv_denom[:, :], denom[:, :]).then_inc(soft_step, 1)
                    dve.wait_ge(soft_step, 2 * i + 2)
                    nc.vector.tensor_tensor(exps[i % 6], exps[i % 6],
                                            inv_denom[:, :].unsqueeze(2).to_broadcast([P, 4, P]), ALU.mult)\
                      .then_inc(probs_done, 1)

                def split_mixed(g):
                    dve.wait_ge(mixed_hi, 2 * g + 2)
                    for qt in range(2):
                        bank = mix_bank(g, qt)
                        part = (slice(None), slice(4 * g, 4 * g + 4), slice(qt * P, (qt + 1) * P))
                        nc.vector.tensor_tensor(y_lo[part], bank, y_hi[part].bitcast(F32), ALU.subtract)\
                          .then_inc(mixed_split, 1)

                q_tiles(0)
                q_tiles(1)
                maxima(0)
                maxima(1)
                normalise(0)
                normalise(1)
                q_tiles(2)
                maxima(2)
                maxima(3)
                normalise(2)
                normalise(3)
                q_tiles(3)
                maxima(4)
                maxima(5)
                normalise(4)
                split_mixed(0)
                maxima(6)
                normalise(5)
                maxima(7)
                normalise(6)
                normalise(7)
                split_after(n0 + 5)
                split_mixed(1)
                split_after(n0 + 6)
                split_after(n0 + 7)

            dve.wait_ge(params_landed, 16)
            for p in range(4):
                dve.wait_ge(x_landed[p], 16)
            ffn(0)
            retention()
            ffn(1)
            ffn(2)
            attention()
            ffn(3)
            norm_input(LAST_NORM, CHUNKS - 1)
            norm_rstd(LAST_NORM)
            for k in range(KT):
                to = (result, result2)[k // 4]
                nc.vector.scalar_tensor_tensor(to[:, k % 4, :], x[:, k, :], gain(LAST_NORM, k), rstd[:, 0:TOKENS],
                                               ALU.mult, ALU.mult).then_inc(result_done, 1)

        @block.tensor
        def _(pe):
            def passes(s, word, width):
                w = slice(word, word + width)
                return (w_hi[:, s, w], "hi"), (w_hi[:, s, w], "lo"), (w_lo[:, s, w], "hi")

            def stats(e):
                pe.wait_ge(sum_done, 3 * e + 3)
                if e == 0:
                    pe.wait_ge(ones_set, 2)
                flat = misc[1][:, :, :].rearrange("p a t -> p (a t)")
                for half in range(2):
                    last = nc.tensor.matmul(flat[:, 0:TOKENS], ones[:, :], sq_sum[:, half, :],
                                            start=(half == 0), stop=(half == 1))
                if e in (RET_NORM, ATT_NORM):
                    for tt in range(2):
                        for half in range(2):
                            last = nc.tensor.matmul(flat[:, TOKENS + tt:TOKENS + tt + 1],
                                                    sq_sum[:, half, tt * P:(tt + 1) * P], ones[:, 0:1],
                                                    start=(half == 0), stop=(half == 1))
                last.then_inc(stats_ready, 1)

            def two_tiles(c, bank, turn=0, norm=None):
                s = c % RING
                if c:
                    pe.wait_ge(split_done, RING * turn + c)
                order = [(t, k) for t in range(2) for k in range(KT)]
                if norm is not None:
                    order = [(t, k) for k in range(KT) for t in range(2)]
                for n, (t, k) in enumerate(order):
                    if norm is not None and t == 0:
                        pe.wait_ge(a_split, 8 * norm + k + 1)
                        if norm == 0 and k % 2 == 0:
                            pe.wait_ge(first_split, k // 2 + 1)
                    if norm is not None and n == 14:
                        stats(norm)
                    for m, (w, part) in enumerate(passes(s, (2 * k + t) * P, P)):
                        first = m == 0 and (n == 0 if norm is not None else k == 0)
                        last = nc.tensor.matmul(bank[:, t, :], w, (a_hi if part == "hi" else a_lo)[:, k, :],
                                                start=first, stop=(m == 2 and k == KT - 1),
                                                skip_group_check=norm is not None)
                last.then_inc(chunk_used, 1)

            def project(c, b_hi, b_lo, first, last_one, turn=0):
                s = c % RING
                if c:
                    pe.wait_ge(split_done, RING * turn + c)
                for d in range(KT):
                    for k in range(2):
                        for m, (w, part) in enumerate(passes(s, (KT * k + d) * P, P)):
                            mm = nc.tensor.matmul(acc[d // 2][:, d % 2, :], w, (b_hi if part == "hi" else b_lo)[:, k, :],
                                                  start=(first and d % 2 == 0 and k == 0 and m == 0),
                                                  stop=(last_one and k == 1 and m == 2), skip_group_check=True)
                    if last_one and d in (1, 3, 5):
                        mm.then_inc(acc_ready, 1)
                mm.then_inc(chunk_used, 1)

            def gate_up_tile(f, jt, turn=0, norm=None):
                t = f * FF_TILES + jt
                if jt >= 2:
                    pe.wait_ge(scaled, 2 * turn + t - 1)
                two_tiles(gate_chunk(f, jt), proj[jt % 2], turn, norm)

            def down(f, pair, buf, turn=0):
                pe.wait_ge(h_split, turn + f * FF_PAIRS + pair + 1)
                project(down_chunk(f, pair), h_hi[:, buf], h_lo[:, buf], pair == 0, pair == FF_PAIRS - 1, turn)

            def ffn(f):
                gate_up_tile(f, 0, norm=FFN_NORM[f])
                gate_up_tile(f, 1)
                for j in (2, 3):
                    gate_up_tile(f, j)
                down(f, 0, 0)
                with pe.Fori(0, FF_PAIRS - 3) as i:
                    for j in (4, 5):
                        gate_up_tile(f, j, i)
                    down(f, 1, 0, i)
                last = FF_TILES - 2
                gate_up_tile(f, last)
                gate_up_tile(f, last + 1)
                down(f, FF_PAIRS - 2, 0)
                down(f, FF_PAIRS - 1, 1)

            def scores(hd):
                pe.wait_ge(rope_sum, 4 * hd + 4)
                if hd >= 2:
                    pe.wait_ge(decay_done, hd - 1)
                flat = misc[hd % 2][:, :, :].rearrange("p a t -> p (a t)")
                for key, (at, q0) in enumerate(((0, 0), (TOKENS, P))):
                    for t in range(2):
                        last = nc.tensor.matmul(flat[:, at:at + TOKENS - q0], qk[:, hd % 2, 1, t, key * P:(key + 1) * P],
                                                qk[:, hd % 2, 0, t, q0:TOKENS], start=(t == 0), stop=(t == 1))
                last.then_inc(scores_ready, 1)

            def head_values(hd):
                for half in range(2):
                    c = v_chunk(hd, half)
                    s = c % RING
                    pe.wait_ge(split_done, c)
                    if hd >= 2 and half == 0:
                        pe.wait_ge(v_kept, 2 * (hd - 1))
                    for tt in range(2):
                        for k in range(4):
                            w = slice(k * RET_V, (k + 1) * RET_V)
                            kk = 4 * half + k
                            tok = slice(tt * P, (tt + 1) * P)
                            for m, (a, b) in enumerate(((a_hi, w_hi), (a_lo, w_hi), (a_hi, w_lo))):
                                last = nc.tensor.matmul(acc[2 * (hd % 2) + tt][:, :, :].rearrange("p a t -> p (a t)"),
                                                        a[:, kk, tok], b[:, s, w],
                                                        start=(kk == 0 and m == 0), stop=(kk == 7 and m == 2),
                                                        skip_group_check=True)
                    last.then_inc(chunk_used, 1)

            def retained(hd):
                pe.wait_ge(decay_done, min(hd + 1, RET_HEADS) if hd else RET_HEADS)
                pe.wait_ge(v_kept, 2 * hd + 2)
                if hd:
                    pe.wait_ge(gn_step, 6 * hd)
                for t in range(V_TILES):
                    w = slice(hd * RET_V + t * P, hd * RET_V + (t + 1) * P)
                    nc.tensor.matmul(misc[t // 2][:, t % 2, :], values[:, 0, w], decayed[:, hd, 0:TOKENS],
                                     start=True, stop=False)
                    last = nc.tensor.matmul(misc[t // 2][:, t % 2, P:TOKENS], values[:, 1, w],
                                            decayed[:, hd, TOKENS:BAND], start=False, stop=True)
                last.then_inc(o_ready, 1)

            def sum_over_values(bank, ready):
                for half in range(2):
                    last = nc.tensor.matmul(bank[:, 0, :], ones[:, :], o_sum[:, half, :],
                                            start=(half == 0), stop=(half == 1))
                last.then_inc(ready, 1)

            def retention():
                for hd in range(RET_HEADS):
                    for which in range(2):
                        if hd:
                            pe.wait_ge(roped, 2 * (2 * (hd - 1) + which) + 2)
                        two_tiles((q_chunk, k_chunk)[which](hd), proj[which],
                                  norm=RET_NORM if hd == which == 0 else None)
                    if hd:
                        if hd == 2:
                            pe.wait_ge(norm_step, 6 * (RET_NORM + 1))
                        scores(hd - 1)
                head_values(0)
                scores(RET_HEADS - 1)
                for hd in range(1, RET_HEADS):
                    head_values(hd)
                for kind, hd in RET_TAIL:
                    if kind == "g":
                        retained(hd)
                        for half in range(2):
                            if hd:
                                pe.wait_ge(g_scaled, 2 * (hd - 1) + half + 1)
                            else:
                                pe.wait_ge(rope_sum, 4 * RET_HEADS)
                            two_tiles(tail_chunk(kind, hd, half), proj[half])
                            pe.wait_ge(o_added, 2 * hd + half + 1)
                            sum_over_values(misc[half], (mean_ready, var_ready)[half])
                    else:
                        pe.wait_ge(y_split, hd + 1)
                        if hd == 0:
                            pe.wait_ge(v_kept, 2 * RET_HEADS)
                        for half in range(2):
                            t = 4 * (hd % 2) + 2 * half
                            project(tail_chunk(kind, hd, half), y_hi[:, t:t + 2, :], y_lo[:, t:t + 2, :],
                                    hd == half == 0, hd == RET_HEADS - 1 and half == 1)

            def attention():
                n0 = ATT_AT
                two_tiles(n0, proj[0], norm=ATT_NORM)
                s = (n0 + 1) % RING
                pe.wait_ge(split_done, n0 + 1)
                for tt in range(2):
                    for k in range(KT):
                        for m, (a, b) in enumerate(((a_hi, w_hi), (a_lo, w_hi), (a_hi, w_lo))):
                            last = nc.tensor.matmul(proj[1][:, tt, :], a[:, k, tt * P:(tt + 1) * P],
                                                    b[:, s, k * 256:(k + 1) * 256],
                                                    start=(k == 0 and m == 0), stop=(k == 7 and m == 2))
                last.then_inc(chunk_used, 1)

                def q_tiles(c):
                    if c == 0:
                        pe.wait_ge(kqv_scaled, 1)
                    elif c == 1:
                        pe.wait_ge(v_done, 2)
                    else:
                        pe.wait_ge(kqv_scaled, c)
                    two_tiles(n0 + 2 + c, proj[c % 2])

                def query_scores(c):
                    pe.wait_ge(q_done, 2 * c + 2)
                    if c == 0:
                        pe.wait_ge(k_done, 2)
                        pe.wait_ge(norm_step, 6 * (ATT_NORM + 1))
                    elif c == 2:
                        pe.wait_ge(exp_done, 10)
                    elif c == 3:
                        pe.wait_ge(kqv_scaled, 5)
                    for f in range(2):
                        rows = slice(HEAD * f, HEAD * f + HEAD)
                        for t in range(2):
                            for n in range(4):
                                k0, width = (0, CHUNK) if n == 0 else (CHUNK * (n - 1), 2 * CHUNK)
                                to = (n // 2) * P
                                half = CHUNK * (n % 2)
                                last = nc.tensor.matmul(scores_bank(2 * c + f)[half:half + CHUNK, t, to:to + width],
                                                        att_q[rows, 2 * c + t, CHUNK * n:CHUNK * n + CHUNK],
                                                        att_k[rows, c // 2, k0:k0 + width], start=True, stop=True)
                        last.then_inc(att_scores, 1)

                def turn_probs(i):
                    pe.wait_ge(probs_done, i + 1)
                    if i == 0:
                        pe.wait_ge(consts_landed, 16)
                    if i >= 2:
                        pe.wait_ge(turned_kept, i - 1)
                    flat = turned_bank(i)[:, :, :].rearrange("p a t -> p (a t)")
                    for b in range(4):
                        last = nc.tensor.transpose(flat[:, b * P:(b + 1) * P], exps[i % 6][:, b, :],
                                                   consts[:, IDENT:IDENT + P])
                    last.then_inc(turned, 1)

                def mix(g):
                    pe.wait_ge(turned_kept, 4 * g + 4)
                    pe.wait_ge(v_shifted, 32)
                    for c in range(4):
                        bank = mix_bank(g, c // 2)
                        tok = (0, 0, 2, 1)[c]
                        for f in range(2):
                            kv = 2 * g + f
                            at = (2 * f + c // 2) * P + (c % 2) * CHUNK
                            last = nc.tensor.matmul(
                                bank[HEAD * f:HEAD * f + HEAD, :, CHUNK * (c % 2):CHUNK * (c % 2) + CHUNK],
                                att_v[:, tok, kv * HEAD:(kv + 1) * HEAD],
                                probs_t[:, 4 * g:4 * g + 4, at:at + CHUNK], start=True, stop=True)
                    last.then_inc(mixed, 1)

                def out_tiles(c):
                    pe.wait_ge(mixed_split, 2 * (c // 2) + 2)
                    project(n0 + 6 + c, y_hi[:, 2 * c:2 * c + 2, :], y_lo[:, 2 * c:2 * c + 2, :], c == 0, c == 3)

                q_tiles(0)
                q_tiles(1)
                query_scores(0)
                q_tiles(2)
                query_scores(1)
                turn_probs(0)
                turn_probs(1)
                q_tiles(3)
                query_scores(2)
                turn_probs(2)
                turn_probs(3)
                mix(0)
                query_scores(3)
                out_tiles(0)
                for u in range(4, 8):
                    turn_probs(u)
                mix(1)
                out_tiles(1)
                out_tiles(2)
                out_tiles(3)

            ffn(0)
            retention()
            ffn(1)
            ffn(2)
            attention()
            ffn(3)
            stats(LAST_NORM)


def laid_out(inputs):
    a = {n: np.asarray(v) for n, v in inputs.items()}

    def columns(w):
        n = w.shape[1] // (2 * P)
        return w.reshape(KT, P, n, 2, P).transpose(2, 1, 0, 3, 4).reshape(n, P, WORDS)

    def rows(w):
        n = w.shape[0] // (2 * P)
        return w.reshape(n, 2, P, KT, P).transpose(0, 2, 1, 3, 4).reshape(n, P, WORDS)

    def ffn(w_in, w_out):
        gate, up = w_in[:, :D_FF].reshape(D_MODEL, FF_TILES, P), w_in[:, D_FF:].reshape(D_MODEL, FF_TILES, P)
        tiles = columns(np.stack([gate, up], 2).reshape(D_MODEL, 2 * D_FF))
        down = rows(w_out)
        order = [tiles[0], tiles[1]]
        for i in range(1, FF_PAIRS):
            order += [tiles[2 * i], tiles[2 * i + 1], down[i - 1]]
        return order + [down[FF_PAIRS - 1]]

    def ret(w_in, w_out):
        q, k, v, g = np.split(w_in, [D_MODEL, 2 * D_MODEL, 4 * D_MODEL], axis=1)
        q, k, g, o = columns(q), columns(k), columns(g), rows(w_out)
        order = []
        for hd in range(RET_HEADS):
            order += [q[hd], k[hd]]
        for hd in range(RET_HEADS):
            for half in range(2):
                part = v[half * 512:(half + 1) * 512, hd * RET_V:(hd + 1) * RET_V]
                order.append(part.reshape(4, P, RET_V).transpose(1, 0, 2).reshape(P, WORDS))
        for which, hd in ((g, 0), (g, 1), (o, 0), (g, 2), (o, 1), (g, 3), (o, 2), (o, 3)):
            order += [which[2 * hd], which[2 * hd + 1]]
        return order

    heads = [8 * (i // 4) + 4 * f + i % 4 for i in range(8) for f in range(2)]
    q_cols = np.concatenate([np.arange(HEAD) + HEAD * n for n in heads])

    def att(w_in, w_out):
        q, k, v = w_in[:, :1024][:, q_cols], w_in[:, 1024:1280], w_in[:, 1280:]
        v = v.reshape(KT, P, 256).transpose(1, 0, 2).reshape(P, WORDS)
        return [columns(k)[0], v, *columns(q), *rows(w_out[q_cols])]

    up1, down1, up2, down2 = (a[n] for n in ("ffn1_w_gate_up", "ffn1_w_down", "ffn2_w_gate_up", "ffn2_w_down"))
    weights = np.stack(ffn(up1[0], down1[0]) + ret(a["ret_w_in"][0], a["ret_w_out"][0]) + ffn(up2[0], down2[0])
                       + ffn(up1[1], down1[1]) + att(a["att_w_in"][0], a["att_w_out"][0]) + ffn(up2[1], down2[1]))

    def by_tile(v):
        return v.reshape(-1, P).T

    norms = [a["ffn1_norm"][0], a["mix_norm"][0], a["ffn2_norm"][0], a["ffn1_norm"][1], a["mix_norm"][1],
             a["ffn2_norm"][1], a["final_norm"]]
    b_in = a["att_b_in"][0]
    sinks = a["att_sinks"][0][np.array(heads)].reshape(4, 2, 2).transpose(0, 2, 1).reshape(-1).repeat(2)
    params = np.concatenate([*map(by_tile, norms), by_tile(a["ret_gn_gain"][0]), by_tile(b_in[:1024][q_cols]),
                             by_tile(b_in[1024:1280]), by_tile(a["att_b_out"][0]),
                             np.broadcast_to(sinks, (P, 32)), np.broadcast_to(b_in[1280:], (P, 256))], axis=1)
    x = a["x"][0].T.reshape(KT, P, TOKENS).transpose(1, 0, 2)
    return {"x_in": x, "weights": weights, "params_in": params, "consts_in": constants()}


def constants():
    f = np.float32
    theta = f(10000.0) ** (-np.linspace(0.0, 1.0, RET_QK // 2, dtype=f))
    angle = np.arange(TOKENS, dtype=f)[None, :] * theta[:, None]
    log_gamma = np.log(1.0 - 2.0 ** (-5.0 - np.arange(RET_HEADS)))
    key, query = np.arange(TOKENS)[:, None], np.arange(TOKENS)[None, :]
    decay = np.exp(log_gamma[:, None, None] * np.abs(query - key)) * (query // CHUNK >= key // CHUNK)
    decay = decay * RET_QK ** -0.5
    band = [np.concatenate([d[:P], d[P:, P:]], axis=1) for d in decay]
    return np.concatenate([np.cos(angle), np.sin(angle), np.eye(P), *band], axis=1).astype(f)


def kernel(**inputs):
    import concourse.bacc as bacc
    from concourse.bass_utils import run_bass_kernel_spmd

    nc = bacc.Bacc("TRN2", target_bir_lowering=False, num_devices=1)
    arrays, args = {}, []
    for name, v in laid_out(inputs).items():
        v = np.ascontiguousarray(v)
        arrays[name] = v
        args.append(nc.dram_tensor(name, v.shape, mybir.dt.from_np(v.dtype), kind="ExternalInput").ap())
    out = nc.dram_tensor("out", (P, KT, TOKENS), F32, kind="ExternalOutput").ap()
    trunk(nc, *args, out)
    r = run_bass_kernel_spmd(nc, [arrays], core_ids=[0])
    got = np.asarray(r.results[0]["out"])
    return np.ascontiguousarray(got.transpose(2, 1, 0).reshape(1, TOKENS, D_MODEL))
```

```python
from contextlib import ExitStack

import numpy as np

import concourse.bass as bass
from concourse import mybir

F32 = mybir.dt.float32
F32R = mybir.dt.float32r
ALU = mybir.AluOpType
ACT = mybir.ActivationFunctionType
AXIS_X = mybir.AxisListType.X

P = 128
TOKENS = 256
D_MODEL = 1024
KT = D_MODEL // P
D_FF = 2816
FF_TILES = D_FF // P
FF_PAIRS = FF_TILES // 2
CHUNK = 64
EPS = 1e-6
RET_HEADS = 4
RET_QK = D_MODEL // RET_HEADS
RET_V = 2 * RET_QK
V_TILES = RET_V // P
Q_HEADS, KV_HEADS, HEAD = 16, 4, 64
WORDS = 2048
RING = 3

FFN_CHUNKS = 3 * FF_PAIRS
RET_CHUNKS = 8 * RET_HEADS
ATT_CHUNKS = 10
FFN_AT = [0, FFN_CHUNKS + RET_CHUNKS, 2 * FFN_CHUNKS + RET_CHUNKS, 3 * FFN_CHUNKS + RET_CHUNKS + ATT_CHUNKS]
RET_AT = FFN_CHUNKS
ATT_AT = 3 * FFN_CHUNKS + RET_CHUNKS
CHUNKS = 4 * FFN_CHUNKS + RET_CHUNKS + ATT_CHUNKS
assert CHUNKS % RING == 0 and FFN_CHUNKS % RING == 0
FFN_NORM, RET_NORM, ATT_NORM, LAST_NORM = [0, 2, 3, 5], 1, 4, 6

GAIN = 0
GN_GAIN = GAIN + 7 * KT
BIAS_Q = GN_GAIN + RET_HEADS * V_TILES
BIAS_K = BIAS_Q + 8
BIAS_OUT = BIAS_K + 2
SINKS = BIAS_OUT + KT
BIAS_V = SINKS + 32
PARAMS = BIAS_V + KV_HEADS * HEAD

COS, SIN = 0, TOKENS
IDENT = 2 * TOKENS
DECAY = IDENT + P
BAND = TOKENS + P
CONSTS = DECAY + RET_HEADS * BAND


def trunk(nc, x_in, weights, params_in, consts_in, out):
    with ExitStack() as ctx:
        def sb(name, shape, dt=F32):
            return ctx.enter_context(nc.sbuf_tensor(name, shape, dt))

        def sem(name):
            return ctx.enter_context(nc.semaphore(name))

        raw = sb("raw", [P, RING, WORDS])
        w_hi = sb("w_hi", [P, RING, WORDS], F32R)
        w_lo = sb("w_lo", [P, RING, WORDS], F32R)
        params = sb("params", [P, PARAMS])
        consts = sb("consts", [P, CONSTS])
        ones = sb("ones", [P, P])
        eps = sb("eps", [P, 1])
        x = sb("x", [P, KT, TOKENS])
        a_hi = sb("a_hi", [P, KT, TOKENS], F32R)
        a_lo = sb("a_lo", [P, KT, TOKENS], F32R)
        sq_sum = sb("sq_sum", [P, 2, TOKENS])
        mean_sq = sb("mean_sq", [P, 2])
        root = sb("root", [P, 2])
        guess = sb("guess", [P, 2])
        newton = sb("newton", [P, 2])
        rstd_col = sb("rstd_col", [P, 2])
        gn_col = sb("gn_col", [P, 2])
        diagonal = sb("diagonal", [P, 2, P])
        rstd = sb("rstd", [P, TOKENS])
        gate_up = sb("gate_up", [P, 2, 2, TOKENS])
        gate_act = sb("gate_act", [P, 2, TOKENS])
        h = sb("h", [P, 2, TOKENS])
        h_hi = sb("h_hi", [P, 2, 2, TOKENS], F32R)
        h_lo = sb("h_lo", [P, 2, 2, TOKENS], F32R)
        cos_r = sb("cos_r", [P, 2, TOKENS])
        rope_a = sb("rope_a", [P, 2, TOKENS])
        rope_b = sb("rope_b", [P, 2, TOKENS])
        qk = sb("qk", [P, 2, 2, 2, TOKENS])
        decayed = sb("decayed", [P, RET_HEADS, BAND])
        values = sb("values", [P, 2, RET_HEADS * RET_V])
        o_head = sb("o_head", [P, V_TILES, TOKENS])
        o_sq = sb("o_sq", [P, V_TILES, TOKENS])
        o_sum = sb("o_sum", [P, 2, TOKENS])
        g_act = sb("g_act", [P, 2, V_TILES, TOKENS])
        x_sq = [buf[:, 2 * n:2 * n + 2, :] for buf in (o_head, o_sq) for n in range(2)]
        y_hi = sb("y_hi", [P, 8, TOKENS], F32R)
        y_lo = sb("y_lo", [P, 8, TOKENS], F32R)
        att_k = rope_a
        att_v = g_act[:, 1, 0:3, :]
        att_q = qk[:, :, :, :, :].rearrange("p a b c t -> p (a b c) t")
        probs_t = values[:, :, :].rearrange("p a (i n) -> p (a i) n", n=4 * P)
        exps = [half.rearrange("p c (d t) -> p (c d) t", d=2)
                for buf in (g_act[:, 0, :, :], o_head, o_sq) for half in (buf[:, 0:2, :], buf[:, 2:4, :])]
        row_max = sb("row_max", [P, 4])
        neg_max = sb("neg_max", [P, 2, 4])
        neg_sinks = sb("neg_sinks", [P, 32])
        sink_arg = sb("sink_arg", [P, 2, 4])
        sink_exp = sb("sink_exp", [P, 2, 4])
        exp_sum = sb("exp_sum", [P, 2, 4])
        denom = sb("denom", [P, 4])
        inv_denom = sb("inv_denom", [P, 4])
        result = [qk[:, a, b] for a in range(2) for b in range(2)]

        banks = [ctx.enter_context(nc.psum_tensor(f"bank{i}", [P, 2, TOKENS], F32)) for i in range(8)]
        acc = banks[0:4]
        proj = banks[4:6]
        misc = banks[6:8]

        x_landed = [sem(f"x_landed{p}") for p in range(4)]
        first_landed = [sem(f"first_landed{q}") for q in range(4)]
        consts_landed = sem("consts_landed")
        first_rounded = sem("first_rounded")
        first_split = sem("first_split")
        params_landed = sem("params_landed")
        raw_landed = [sem(f"raw_landed{s}") for s in range(RING)]
        ones_set = sem("ones_set")
        hi_done = sem("hi_done")
        split_done = sem("split_done")
        chunk_used = sem("chunk_used")
        acc_ready = sem("acc_ready")
        x_new = sem("x_new")
        a_hi_done = sem("a_hi_done")
        a_split = sem("a_split")
        sq_done = sem("sq_done")
        sum_done = sem("sum_done")
        stats_ready = sem("stats_ready")
        ident_landed = sem("ident_landed")
        diag_done = sem("diag_done")
        spread_ready = sem("spread_ready")
        rstd_done = sem("rstd_done")
        root_done = sem("root_done")
        norm_step = sem("norm_step")
        scaled = sem("scaled")
        gated = sem("gated")
        h_done = sem("h_done")
        h_hi_done = sem("h_hi_done")
        h_split = sem("h_split")
        tables_ready = sem("tables_ready")
        roped = sem("roped")
        rope_sum = sem("rope_sum")
        scores_ready = sem("scores_ready")
        decay_done = sem("decay_done")
        v_kept = sem("v_kept")
        o_ready = sem("o_ready")
        o_kept = sem("o_kept")
        o_added = sem("o_added")
        mean_ready = sem("mean_ready")
        centred = sem("centred")
        o_gated = sem("o_gated")
        sinks_ready = sem("sinks_ready")
        o_squared = sem("o_squared")
        g_scaled = sem("g_scaled")
        g_done = sem("g_done")
        y_done = sem("y_done")
        y_hi_done = sem("y_hi_done")
        y_split = sem("y_split")
        kqv_scaled = sem("kqv_scaled")
        k_done = sem("k_done")
        v_done = sem("v_done")
        v_shifted = sem("v_shifted")
        q_done = sem("q_done")
        att_scores = sem("att_scores")
        masked = sem("masked")
        max_step = sem("max_step")
        exp_done = sem("exp_done")
        soft_step = sem("soft_step")
        probs_done = sem("probs_done")
        turned = sem("turned")
        turned_kept = sem("turned_kept")
        mixed = sem("mixed")
        mixed_hi = sem("mixed_hi")
        mixed_split = sem("mixed_split")
        result_done = sem("result_done")
        stored = sem("stored")

        def scores_bank(u):
            return (misc, acc[2:4], misc, proj)[u // 2][u % 2]

        def turned_bank(u):
            return (acc, acc, misc, proj)[u // 2][u % 2]

        def mix_bank(g, qt):
            bank = (acc[2:4] if g == 0 else misc)[qt]
            return bank[:, :, :].rearrange("p a (b t) -> p (a b) t", t=P)

        def used(c):
            return c + 1

        def gate_chunk(f, j):
            return FFN_AT[f] + (j if j < 2 else 2 + 3 * (j // 2 - 1) + j % 2)

        def down_chunk(f, i):
            return FFN_AT[f] + (4 + 3 * i if i < FF_PAIRS - 1 else FFN_CHUNKS - 1)

        def gain(e, k):
            return params[:, GAIN + e * KT + k:GAIN + e * KT + k + 1]

        def row_rstd():
            return rstd[:, :].unsqueeze(1).to_broadcast([P, 2, TOKENS])

        def nth_norm(e):
            return e + (RET_HEADS if e > RET_NORM else 0)

        def nth_head(hd):
            return RET_NORM + 1 + hd

        def stats_bank(n):
            return acc[3] if n == nth_head(0) else misc[1]

        def mean_bank(hd):
            return acc[2] if hd == 0 else misc[0]

        def q_chunk(hd):
            return RET_AT + 2 * hd

        def k_chunk(hd):
            return RET_AT + 2 * hd + 1

        def v_chunk(hd, half):
            return RET_AT + 2 * RET_HEADS + 2 * hd + half

        RET_TAIL = [("g", 0), ("g", 1), ("o", 0), ("g", 2), ("o", 1), ("g", 3), ("o", 2), ("o", 3)]

        def tail_chunk(kind, hd, half):
            return RET_AT + 4 * RET_HEADS + 2 * RET_TAIL.index((kind, hd)) + half

        def quarter(q):
            return slice(q * WORDS // 4, (q + 1) * WORDS // 4)

        block = ctx.enter_context(nc.Block())

        @block.sync
        def _(sp):
            sp.dma_start(params[:, :], params_in).then_inc(params_landed, 16)
            for p in range(4):
                sp.dma_start(x[:, 2 * p:2 * p + 2, :], x_in[:, 2 * p:2 * p + 2, :]).then_inc(x_landed[p], 16)
            sp.dma_start(consts[:, IDENT:DECAY], consts_in[:, IDENT:DECAY]).then_inc(ident_landed, 16)
            for s in range(1, RING):
                sp.dma_start(raw[:, s, :], weights[s]).then_inc(raw_landed[s], 16)
            for part in (slice(0, IDENT), slice(DECAY, CONSTS)):
                sp.dma_start(consts[:, part], consts_in[:, part]).then_inc(consts_landed, 16)
            with sp.Fori(1, CHUNKS // RING) as turn:
                for s in range(RING):
                    sp.wait_ge(split_done, turn * RING + max(s - RING, 1 - RING))
                    sp.dma_start(raw[:, s, :], weights[bass.ds(turn * RING + s, 1)].rearrange("o p w -> (o p) w"))\
                      .then_inc(raw_landed[s], 16)
            for p in range(4):
                sp.wait_ge(result_done, p + 1)
                sp.dma_start(out[:, 2 * p:2 * p + 2, :], result[p]).then_inc(stored, 16)
            sp.wait_ge(stored, 64)

        @block.gpsimd
        def _(pool):
            nc.gpsimd.memset(ones[:, :], 1.0).then_inc(ones_set, 1)
            nc.gpsimd.memset(eps[:, :], EPS).then_inc(ones_set, 1)
            for e in range(LAST_NORM):
                if e:
                    pool.wait_ge(stats_ready, nth_norm(e - 1) + 1)
                for p in range(1, 4):
                    pool.wait_ge(sq_done, 4 * e + p + 1)
                    if p > 1:
                        pool.wait_ge(sum_done, 3 * e + p - 1)
                    first = x_sq[0] if p == 1 else sq_sum[:, :, :]
                    nc.gpsimd.tensor_tensor(sq_sum[:, :, :], first, x_sq[p], ALU.add).then_inc(sum_done, 1)

        @block.scalar
        def _(act):
            def round_chunk(c, turn=0):
                s = c % RING
                act.wait_ge(raw_landed[s], 16 * turn + 16 * (c // RING + (1 if s else 0)))
                if c >= RING:
                    act.wait_ge(chunk_used, RING * turn + used(c - RING))
                nc.scalar.activation(w_hi[:, s, :], raw[:, s, :], ACT.Copy).then_inc(hi_done, 1)

            def round_after(c, turn=0):
                if c + RING < CHUNKS:
                    round_chunk(c + RING, turn)

            def norm_input(e):
                def square(p):
                    if e and p == 0:
                        act.wait_ge(sum_done, 3 * e)
                    nc.scalar.activation(x_sq[p], x[:, 2 * p:2 * p + 2, :], ACT.Square).then_inc(sq_done, 1)

                for p in range(4):
                    if e:
                        act.wait_ge(x_new, 4 * (e - 1) + p + 1)
                    else:
                        act.wait_ge(first_landed[p], 16)
                        nc.scalar.activation(w_hi[:, 0, quarter(p)], raw[:, 0, quarter(p)], ACT.Copy)\
                          .then_inc(first_rounded, 1)
                        act.wait_ge(x_landed[p], 16)
                    if e < LAST_NORM:
                        for k in (2 * p, 2 * p + 1):
                            nc.scalar.activation(a_hi[:, k, :], x[:, k, :], ACT.Copy, scale=gain(e, k))\
                              .then_inc(a_hi_done, 1)
                    if e:
                        square(p)
                if e == 0:
                    round_chunk(1)
                    for p in range(4):
                        square(p)
                    round_chunk(2)

            def root_of(n, scale):
                act.wait_ge(stats_ready, n + 1)
                if n:
                    act.wait_ge(norm_step, 6 * n)
                nc.scalar.activation(root[:, :], stats_bank(n)[:, 1, 0:2], ACT.Sqrt, scale=scale,
                                     bias=eps[:, :]).then_inc(root_done, 1)

            def norm_root(e):
                root_of(nth_norm(e), 1.0 / D_MODEL)

            def gate_tile(f, jt, i=0):
                t = f * FF_TILES + jt
                act.wait_ge(scaled, 2 * i + t + 1)
                if t >= 2:
                    act.wait_ge(h_done, 2 * i + t - 1)
                nc.scalar.activation(gate_act[:, jt % 2, :], gate_up[:, jt % 2, 0, :], ACT.Silu).then_inc(gated, 1)

            def round_h(f, pair, buf, i=0):
                t = f * FF_PAIRS + pair
                act.wait_ge(h_done, 2 * i + 2 * t + 2)
                nc.scalar.activation(h_hi[:, buf], h[:, :, :], ACT.Copy).then_inc(h_hi_done, 1)

            def ffn(f):
                n0 = FFN_AT[f]
                norm_input(FFN_NORM[f])
                if n0:
                    round_after(n0 - 2)
                norm_root(FFN_NORM[f])
                if n0:
                    round_after(n0 - 1)
                for j in range(2):
                    round_after(n0 + j)
                    gate_tile(f, j)
                round_h(f, 0, 0)
                with act.Fori(0, FF_PAIRS - 2) as i:
                    for j in (2, 3):
                        round_after(gate_chunk(f, j), i)
                        gate_tile(f, j, i)
                    act.wait_ge(chunk_used, RING * i + used(down_chunk(f, 0)))
                    round_h(f, 1, 0, i)
                    round_after(down_chunk(f, 0), i)
                last = FF_TILES - 2
                round_after(gate_chunk(f, last))
                gate_tile(f, last)
                gate_tile(f, last + 1)
                round_h(f, FF_PAIRS - 1, 1)
                round_after(gate_chunk(f, last + 1))

            def retention():
                norm_input(RET_NORM)
                round_after(RET_AT - 2)
                norm_root(RET_NORM)
                round_after(RET_AT - 1)
                for c in range(q_chunk(0), v_chunk(0, 0)):
                    round_after(c)
                for hd in range(RET_HEADS):
                    round_after(v_chunk(hd, 0))
                    act.wait_ge(chunk_used, used(v_chunk(hd, 1)))
                    act.wait_ge(norm_step, 6 * (nth_norm(RET_NORM) + 1))
                    for tt in range(2):
                        nc.scalar.activation(values[:, tt, hd * RET_V:(hd + 1) * RET_V],
                                             acc[2 * (hd % 2) + tt][:, :, :].rearrange("p a t -> p (a t)"), ACT.Copy,
                                             scale=rstd_col[:, tt:tt + 1]).then_inc(v_kept, 1)
                    round_after(v_chunk(hd, 1))

                def silu_of_gates(hd, half):
                    act.wait_ge(g_scaled, 2 * hd + half + 1)
                    nc.scalar.activation(g_act[:, hd % 2, 2 * half:2 * half + 2, :], gate_up[:, half], ACT.Silu)\
                      .then_inc(g_done, 1)

                for kind, hd in RET_TAIL:
                    if kind == "g":
                        act.wait_ge(o_ready, hd + 1)
                        if hd:
                            act.wait_ge(y_done, 2 * hd)
                        for half in range(2):
                            nc.scalar.activation(o_head[:, 2 * half:2 * half + 2, :], misc[half][:, :, :], ACT.Copy)\
                              .then_inc(o_kept, 1)
                    for half in range(2):
                        c = tail_chunk(kind, hd, half)
                        if kind == "o":
                            if c < RET_AT + RET_CHUNKS - 2:
                                round_after(c)
                        elif half == 0:
                            round_after(c)
                            silu_of_gates(hd, half)
                            act.wait_ge(centred, hd + 1)
                            if hd:
                                act.wait_ge(y_split, 2 * hd)
                            nc.scalar.activation(o_sq[:, :, :], o_head[:, :, :], ACT.Square).then_inc(o_squared, 1)
                        else:
                            silu_of_gates(hd, half)
                            root_of(nth_head(hd), 1.0 / RET_V)
                            round_after(c)
                            if hd >= 2:
                                act.wait_ge(chunk_used, used(tail_chunk("o", hd - 2, 1)))
                            for two in range(2):
                                t = 4 * (hd % 2) + 2 * two
                                act.wait_ge(y_done, 2 * hd + two + 1)
                                nc.scalar.activation(y_hi[:, t:t + 2, :], o_sq[:, 2 * two:2 * two + 2, :],
                                                     ACT.Copy).then_inc(y_hi_done, 1)

            def attention():
                n0 = ATT_AT
                norm_input(ATT_NORM)
                round_after(n0 - 2)
                norm_root(ATT_NORM)
                round_after(n0 - 1)
                round_after(n0)
                for t in range(2):
                    act.wait_ge(kqv_scaled, 1)
                    nc.scalar.activation(att_k[:, t, :], gate_up[:, 0, t, :], ACT.Identity,
                                         bias=params[:, BIAS_K + t:BIAS_K + t + 1]).then_inc(k_done, 1)
                round_after(n0 + 1)
                act.wait_ge(v_done, 2)
                act.dma_start(att_v[0:64, 2, :], att_v[64:128, 0, :]).then_inc(v_shifted, 16)
                act.dma_start(att_v[64:128, 2, :], att_v[0:64, 1, :]).then_inc(v_shifted, 16)

                def q_tiles(c):
                    if c < 3:
                        round_after(n0 + 2 + c)
                    act.wait_ge(kqv_scaled, 2 + c)
                    for t in range(2):
                        q = 2 * c + t
                        nc.scalar.activation(att_q[:, q, :], gate_up[:, (c + 1) % 2, t, :], ACT.Identity,
                                             bias=params[:, BIAS_Q + q:BIAS_Q + q + 1]).then_inc(q_done, 1)

                def exp_tile(i):
                    act.wait_ge(max_step, 3 * i + 3)
                    if i >= 6:
                        act.wait_ge(turned, i - 5)
                    if i >= 2:
                        act.wait_ge(soft_step, 2 * i - 3)
                    for b in range(4):
                        nc.scalar.activation(exps[i % 6][:, b, :], scores_bank(i)[:, b // 2, (b % 2) * P:(b % 2 + 1) * P],
                                             ACT.Exp, scale=HEAD ** -0.5, bias=neg_max[:, i % 2, b:b + 1],
                                             accum_out=exp_sum[:, i % 2, b:b + 1]).then_inc(exp_done, 1)
                    nc.scalar.activation(sink_exp[:, i % 2, :], sink_arg[:, i % 2, :], ACT.Exp).then_inc(exp_done, 1)

                def keep_turned(i):
                    act.wait_ge(turned, i + 1)
                    c, f = i // 2, i % 2
                    nc.scalar.activation(probs_t[:, 2 * c:2 * c + 2, 2 * f * P:(2 * f + 2) * P],
                                         turned_bank(i)[:, :, :], ACT.Copy).then_inc(turned_kept, 1)

                def round_mixed(g):
                    act.wait_ge(mixed, g + 1)
                    for qt in range(2):
                        nc.scalar.activation(y_hi[:, 4 * g:4 * g + 4, qt * P:(qt + 1) * P],
                                             mix_bank(g, qt), ACT.Copy).then_inc(mixed_hi, 1)

                q_tiles(0)
                q_tiles(1)
                exp_tile(0)
                exp_tile(1)
                q_tiles(2)
                exp_tile(2)
                exp_tile(3)
                keep_turned(0)
                keep_turned(1)
                q_tiles(3)
                keep_turned(2)
                keep_turned(3)
                exp_tile(4)
                round_mixed(0)
                exp_tile(5)
                exp_tile(6)
                exp_tile(7)
                round_after(n0 + 5)
                for u in range(4, 8):
                    keep_turned(u)
                round_mixed(1)
                round_after(n0 + 6)
                round_after(n0 + 7)

            for q in range(4):
                act.dma_start(raw[:, 0, quarter(q)], weights[0, :, quarter(q)]).then_inc(first_landed[q], 16)
            act.wait_ge(params_landed, 16)
            act.wait_ge(ones_set, 2)
            ffn(0)
            retention()
            ffn(1)
            ffn(2)
            attention()
            ffn(3)
            norm_input(LAST_NORM)
            norm_root(LAST_NORM)

        @block.vector
        def _(dve):
            def split_chunk(c, turn=0):
                s = c % RING
                dve.wait_ge(hi_done, RING * turn + c)
                nc.vector.tensor_tensor(w_lo[:, s, :], raw[:, s, :], w_hi[:, s, :].bitcast(F32), ALU.subtract)\
                  .then_inc(split_done, 1)

            def split_after(c, turn=0):
                if c + RING < CHUNKS:
                    split_chunk(c + RING, turn)

            def pair_ready(e, p, last_chunk):
                if p < 3:
                    dve.wait_ge(acc_ready, 3 * (e - 1) + p + 1)
                else:
                    dve.wait_ge(chunk_used, used(last_chunk))

            def residual(e, p, last_chunk):
                pair_ready(e, p, last_chunk)
                two = slice(2 * p, 2 * p + 2)
                if e == ATT_NORM + 1:
                    for d in (2 * p, 2 * p + 1):
                        last = nc.vector.scalar_tensor_tensor(x[:, d, :], acc[p][:, d % 2, :],
                                                              params[:, BIAS_OUT + d:BIAS_OUT + d + 1], x[:, d, :],
                                                              ALU.add, ALU.add)
                    last.then_inc(x_new, 1)
                else:
                    factor = 1.0 if e == RET_NORM + 1 else 0.5
                    nc.vector.scalar_tensor_tensor(x[:, two, :], acc[p][:, :, :], factor, x[:, two, :],
                                                   ALU.mult, ALU.add).then_inc(x_new, 1)

            def norm_input(e, last_chunk):
                def split_pair(p):
                    if e == 0:
                        dve.wait_ge(first_rounded, p + 1)
                        nc.vector.tensor_tensor(w_lo[:, 0, quarter(p)], raw[:, 0, quarter(p)],
                                                w_hi[:, 0, quarter(p)].bitcast(F32), ALU.subtract)\
                          .then_inc(first_split, 1)
                    for k in (2 * p, 2 * p + 1):
                        dve.wait_ge(a_hi_done, 8 * e + k + 1)
                        nc.vector.scalar_tensor_tensor(a_lo[:, k, :], x[:, k, :], gain(e, k),
                                                       a_hi[:, k, :].bitcast(F32), ALU.mult, ALU.subtract)\
                          .then_inc(a_split, 1)

                for p in range(4):
                    if e:
                        residual(e, p, last_chunk)
                    if e < LAST_NORM and p:
                        split_pair(p - 1)
                if e < LAST_NORM:
                    split_pair(3)
                if e == 0:
                    for c in range(1, RING):
                        split_chunk(c)

            def inverse_root(n, scale, target):
                base = 6 * n
                dve.wait_ge(root_done, n + 1)
                nc.vector.tensor_scalar(mean_sq[:, :], stats_bank(n)[:, 1, 0:2], scale, EPS, ALU.mult, ALU.add)\
                  .then_inc(norm_step, 1)
                nc.vector.reciprocal(guess[:, :], root[:, :]).then_inc(norm_step, 1)
                dve.wait_ge(norm_step, base + 2)
                nc.vector.tensor_tensor(newton[:, :], guess[:, :], guess[:, :], ALU.mult).then_inc(norm_step, 1)
                dve.wait_ge(norm_step, base + 3)
                nc.vector.tensor_tensor(newton[:, :], newton[:, :], mean_sq[:, :], ALU.mult).then_inc(norm_step, 1)
                dve.wait_ge(norm_step, base + 4)
                nc.vector.tensor_scalar(newton[:, :], newton[:, :], -0.5, 1.5, ALU.mult, ALU.add)\
                  .then_inc(norm_step, 1)
                dve.wait_ge(norm_step, base + 5)
                nc.vector.tensor_tensor(target[:, :], guess[:, :], newton[:, :], ALU.mult).then_inc(norm_step, 1)
                dve.wait_ge(norm_step, base + 6)
                if n == 0:
                    dve.wait_ge(ident_landed, 16)
                for tt in range(2):
                    nc.vector.tensor_scalar(diagonal[:, tt, :], consts[:, IDENT:IDENT + P], target[:, tt:tt + 1], None,
                                            ALU.mult).then_inc(diag_done, 1)

            def norm_rstd(e):
                inverse_root(nth_norm(e), 1.0 / D_MODEL, rstd_col)

            def keep_rstd(e):
                dve.wait_ge(spread_ready, nth_norm(e) + 1)
                nc.vector.tensor_copy(rstd[:, :], misc[1][:, 0, :]).then_inc(rstd_done, 1)
                dve.wait_ge(rstd_done, e + 1)

            def scale_tile(f, jt, i=0):
                t = f * FF_TILES + jt
                dve.wait_ge(chunk_used, RING * i + used(gate_chunk(f, jt)))
                if t >= 2:
                    dve.wait_ge(h_done, 2 * i + t - 1)
                    dve.wait_ge(gated, 2 * i + t - 1)
                nc.vector.tensor_tensor(gate_up[:, jt % 2], proj[jt % 2][:, :, :], row_rstd(), ALU.mult)\
                  .then_inc(scaled, 1)

            def h_tile(f, jt, i=0):
                t = f * FF_TILES + jt
                dve.wait_ge(gated, 2 * i + t + 1)
                if t >= 2:
                    dve.wait_ge(h_split, i + (t // 2))
                nc.vector.tensor_tensor(h[:, jt % 2, :], gate_act[:, jt % 2, :], gate_up[:, jt % 2, 1, :], ALU.mult)\
                  .then_inc(h_done, 1)

            def split_h(f, pair, buf, i=0):
                t = f * FF_PAIRS + pair
                dve.wait_ge(h_hi_done, i + t + 1)
                dve.wait_ge(h_done, 2 * i + 2 * t + 2)
                nc.vector.tensor_tensor(h_lo[:, buf], h[:, :, :], h_hi[:, buf].bitcast(F32), ALU.subtract)\
                  .then_inc(h_split, 1)

            def ffn(f):
                n0 = FFN_AT[f]
                norm_input(FFN_NORM[f], n0 - 1)
                if n0:
                    split_after(n0 - 2)
                norm_rstd(FFN_NORM[f])
                if n0:
                    split_after(n0 - 1)
                keep_rstd(FFN_NORM[f])
                for j in range(2):
                    scale_tile(f, j)
                    split_after(n0 + j)
                    h_tile(f, j)
                split_h(f, 0, 0)
                with dve.Fori(0, FF_PAIRS - 2) as i:
                    for j in (2, 3):
                        scale_tile(f, j, i)
                        split_after(gate_chunk(f, j), i)
                        h_tile(f, j, i)
                    split_h(f, 1, 0, i)
                    split_after(down_chunk(f, 0), i)
                last = FF_TILES - 2
                scale_tile(f, last)
                split_after(gate_chunk(f, last))
                h_tile(f, last)
                scale_tile(f, last + 1)
                h_tile(f, last + 1)
                split_h(f, FF_PAIRS - 1, 1)
                split_after(gate_chunk(f, last + 1))

            def rope(hd, which):
                c = (q_chunk, k_chunk)[which](hd)
                done = 2 * hd + which
                dve.wait_ge(chunk_used, used(c))
                if done:
                    dve.wait_ge(rope_sum, 2 * done)
                two = [cos_r[:, t, :].unsqueeze(1).to_broadcast([P, 2, TOKENS]) for t in range(2)]
                nc.vector.tensor_tensor(rope_a[:, :, :], proj[which][:, :, :], two[0], ALU.mult).then_inc(roped, 1)
                nc.vector.tensor_tensor(rope_b[:, :, :], proj[which][:, :, :], two[1], ALU.mult).then_inc(roped, 1)
                dve.wait_ge(roped, 2 * done + 2)
                if hd >= 2:
                    dve.wait_ge(scores_ready, hd - 1)
                nc.vector.tensor_tensor(qk[:, hd % 2, which, 0, :], rope_a[:, 0, :], rope_b[:, 1, :], ALU.subtract)\
                  .then_inc(rope_sum, 1)
                nc.vector.tensor_tensor(qk[:, hd % 2, which, 1, :], rope_b[:, 0, :], rope_a[:, 1, :], ALU.add)\
                  .then_inc(rope_sum, 1)

            def decay(hd):
                dve.wait_ge(scores_ready, hd + 1)
                nc.vector.tensor_tensor(decayed[:, hd, :], misc[hd % 2][:, :, :].rearrange("p a t -> p (a t)")[:, 0:BAND],
                                        consts[:, DECAY + hd * BAND:DECAY + (hd + 1) * BAND], ALU.mult)\
                  .then_inc(decay_done, 1)

            def gate_values(hd):
                dve.wait_ge(g_done, 2 * hd + 2)
                for t in range(V_TILES):
                    n = GN_GAIN + hd * V_TILES + t
                    nc.vector.scalar_tensor_tensor(o_head[:, t, :], o_head[:, t, :], params[:, n:n + 1],
                                                   g_act[:, hd % 2, t, :], ALU.mult, ALU.mult).then_inc(o_gated, 1)

            def group_norm(hd):
                dve.wait_ge(spread_ready, nth_head(hd) + 1)
                dve.wait_ge(o_gated, 4 * hd + 4)
                row = stats_bank(nth_head(hd))[:, 0, :].unsqueeze(1).to_broadcast([P, 2, TOKENS])
                for two in range(2):
                    part = slice(2 * two, 2 * two + 2)
                    nc.vector.tensor_tensor(o_sq[:, part, :], o_head[:, part, :], row, ALU.mult).then_inc(y_done, 1)
                for two in range(2):
                    t = 4 * (hd % 2) + 2 * two
                    dve.wait_ge(y_hi_done, 2 * hd + two + 1)
                    nc.vector.tensor_tensor(y_lo[:, t:t + 2, :], o_sq[:, 2 * two:2 * two + 2, :],
                                            y_hi[:, t:t + 2, :].bitcast(F32), ALU.subtract).then_inc(y_split, 1)

            def retention():
                norm_input(RET_NORM, RET_AT - 1)
                split_after(RET_AT - 2)
                norm_rstd(RET_NORM)
                split_after(RET_AT - 1)
                keep_rstd(RET_NORM)
                dve.wait_ge(consts_landed, 32)
                for t in range(2):
                    nc.vector.tensor_tensor(cos_r[:, t, :], consts[:, COS + t * TOKENS:COS + (t + 1) * TOKENS],
                                            rstd[:, :], ALU.mult).then_inc(tables_ready, 1)
                dve.wait_ge(tables_ready, 2)
                for hd in range(RET_HEADS):
                    for which in range(2):
                        rope(hd, which)
                        if hd and which == 0:
                            decay(hd - 1)
                        split_after((q_chunk, k_chunk)[which](hd))
                for hd in range(RET_HEADS):
                    split_after(v_chunk(hd, 0))
                    if hd == 0:
                        decay(RET_HEADS - 1)
                    split_after(v_chunk(hd, 1))
                for kind, hd in RET_TAIL:
                    for half in range(2):
                        c = tail_chunk(kind, hd, half)
                        if kind == "g":
                            if half == 0:
                                dve.wait_ge(o_kept, 2 * hd + 2)
                                nc.vector.tensor_tensor(o_sum[:, :, :], o_head[:, 0:2, :], o_head[:, 2:4, :], ALU.add)\
                                  .then_inc(o_added, 1)
                            dve.wait_ge(chunk_used, used(c))
                            dve.wait_ge(h_done, FF_TILES)
                            if hd:
                                dve.wait_ge(g_done, 2 * hd + half - 1)
                            nc.vector.tensor_tensor(gate_up[:, half], proj[half][:, :, :], row_rstd(), ALU.mult)\
                              .then_inc(g_scaled, 1)
                            if half == 0:
                                dve.wait_ge(mean_ready, hd + 1)
                                mean = mean_bank(hd)[:, 0, :].unsqueeze(1).to_broadcast([P, V_TILES, TOKENS])
                                nc.vector.scalar_tensor_tensor(o_head[:, :, :], mean, -1.0 / RET_V, o_head[:, :, :],
                                                               ALU.mult, ALU.add).then_inc(centred, 1)
                                split_after(c)
                                dve.wait_ge(o_squared, hd + 1)
                                nc.vector.tensor_tensor(o_sum[:, :, :], o_sq[:, 0:2, :], o_sq[:, 2:4, :], ALU.add)\
                                  .then_inc(o_added, 1)
                            else:
                                gate_values(hd)
                                inverse_root(nth_head(hd), 1.0 / RET_V, gn_col)
                                split_after(c)
                                group_norm(hd)
                        elif c < RET_AT + RET_CHUNKS - 2:
                            split_after(c)

            def attention():
                n0 = ATT_AT
                norm_input(ATT_NORM, n0 - 1)
                split_after(n0 - 2)
                norm_rstd(ATT_NORM)
                split_after(n0 - 1)
                keep_rstd(ATT_NORM)
                nc.vector.tensor_scalar(neg_sinks[:, :], params[:, SINKS:SINKS + 32], -1.0, None, ALU.mult)\
                  .then_inc(sinks_ready, 1)
                dve.wait_ge(sinks_ready, 1)
                dve.wait_ge(chunk_used, used(n0))
                nc.vector.tensor_tensor(gate_up[:, 0], proj[0][:, :, :], row_rstd(), ALU.mult).then_inc(kqv_scaled, 1)
                split_after(n0)
                dve.wait_ge(chunk_used, used(n0 + 1))
                for tt in range(2):
                    nc.vector.scalar_tensor_tensor(att_v[:, tt, :], proj[1][:, tt, :],
                                                   rstd_col[:, tt:tt + 1],
                                                   params[:, BIAS_V:BIAS_V + KV_HEADS * HEAD], ALU.mult, ALU.add)\
                      .then_inc(v_done, 1)
                split_after(n0 + 1)

                def q_tiles(c):
                    dve.wait_ge(chunk_used, used(n0 + 2 + c))
                    if c == 1:
                        dve.wait_ge(k_done, 2)
                    if c >= 2:
                        dve.wait_ge(q_done, 2 * (c - 1))
                    nc.vector.tensor_tensor(gate_up[:, (c + 1) % 2], proj[c % 2][:, :, :], row_rstd(), ALU.mult)\
                      .then_inc(kqv_scaled, 1)
                    if c < 3:
                        split_after(n0 + 2 + c)

                def maxima(i):
                    dve.wait_ge(att_scores, i + 1)
                    bank = scores_bank(i)[:, :, :].rearrange("p a t -> p (a t)")
                    nc.vector.memset(scores_bank(i)[0:64, :, 64:128], -3.0e38).then_inc(masked, 1)
                    dve.wait_ge(masked, i + 1)
                    nc.vector.tensor_reduce(row_max[:, :], bank.rearrange("p (b t) -> p b t", t=P), AXIS_X, ALU.max)\
                      .then_inc(max_step, 1)
                    dve.wait_ge(max_step, 3 * i + 1)
                    if i >= 2:
                        dve.wait_ge(exp_done, 5 * (i - 1))
                    sinks = neg_sinks[:, 4 * i:4 * i + 4]
                    nc.vector.scalar_tensor_tensor(neg_max[:, i % 2, :], row_max[:, :], -HEAD ** -0.5, sinks,
                                                   ALU.mult, ALU.min).then_inc(max_step, 1)
                    dve.wait_ge(max_step, 3 * i + 2)
                    nc.vector.tensor_tensor(sink_arg[:, i % 2, :], neg_max[:, i % 2, :], sinks, ALU.subtract)\
                      .then_inc(max_step, 1)

                def normalise(i):
                    dve.wait_ge(exp_done, 5 * i + 5)
                    nc.vector.tensor_tensor(denom[:, :], exp_sum[:, i % 2, :], sink_exp[:, i % 2, :], ALU.add)\
                      .then_inc(soft_step, 1)
                    dve.wait_ge(soft_step, 2 * i + 1)
                    nc.vector.reciprocal(inv_denom[:, :], denom[:, :]).then_inc(soft_step, 1)
                    dve.wait_ge(soft_step, 2 * i + 2)
                    nc.vector.tensor_tensor(exps[i % 6], exps[i % 6],
                                            inv_denom[:, :].unsqueeze(2).to_broadcast([P, 4, P]), ALU.mult)\
                      .then_inc(probs_done, 1)

                def split_mixed(g):
                    dve.wait_ge(mixed_hi, 2 * g + 2)
                    for qt in range(2):
                        bank = mix_bank(g, qt)
                        part = (slice(None), slice(4 * g, 4 * g + 4), slice(qt * P, (qt + 1) * P))
                        nc.vector.tensor_tensor(y_lo[part], bank, y_hi[part].bitcast(F32), ALU.subtract)\
                          .then_inc(mixed_split, 1)

                q_tiles(0)
                q_tiles(1)
                maxima(0)
                maxima(1)
                normalise(0)
                normalise(1)
                q_tiles(2)
                maxima(2)
                maxima(3)
                normalise(2)
                normalise(3)
                q_tiles(3)
                maxima(4)
                maxima(5)
                normalise(4)
                split_mixed(0)
                maxima(6)
                normalise(5)
                maxima(7)
                normalise(6)
                normalise(7)
                split_after(n0 + 5)
                split_mixed(1)
                split_after(n0 + 6)
                split_after(n0 + 7)

            dve.wait_ge(params_landed, 16)
            for p in range(4):
                dve.wait_ge(x_landed[p], 16)
            ffn(0)
            retention()
            ffn(1)
            ffn(2)
            attention()
            ffn(3)
            norm_input(LAST_NORM, CHUNKS - 1)
            norm_rstd(LAST_NORM)
            dve.wait_ge(spread_ready, nth_norm(LAST_NORM) + 1)
            for p in range(4):
                for k in (2 * p, 2 * p + 1):
                    last = nc.vector.scalar_tensor_tensor(result[p][:, k % 2, :], x[:, k, :], gain(LAST_NORM, k),
                                                          misc[1][:, 0, :], ALU.mult, ALU.mult)
                last.then_inc(result_done, 1)

        @block.tensor
        def _(pe):
            def passes(s, word, width):
                w = slice(word, word + width)
                return (w_hi[:, s, w], "hi"), (w_hi[:, s, w], "lo"), (w_lo[:, s, w], "hi")

            def sums(n, parts):
                for tt in range(2):
                    for m, part in enumerate(parts):
                        last = nc.tensor.matmul(stats_bank(n)[:, 1, tt:tt + 1], part[:, tt * P:(tt + 1) * P],
                                                ones[:, 0:1], start=(m == 0), stop=(m == len(parts) - 1))
                last.then_inc(stats_ready, 1)

            def stats(e):
                if e == LAST_NORM:
                    pe.wait_ge(sq_done, 4 * LAST_NORM + 4)
                    sums(nth_norm(e), [x_sq[p][:, half, :] for p in range(4) for half in range(2)])
                    return
                pe.wait_ge(sum_done, 3 * e + 3)
                if e == 0:
                    pe.wait_ge(ones_set, 2)
                sums(nth_norm(e), [sq_sum[:, half, :] for half in range(2)])

            def spread(n):
                pe.wait_ge(diag_done, 2 * n + 2)
                for tt in range(2):
                    last = nc.tensor.matmul(stats_bank(n)[:, 0, tt * P:(tt + 1) * P], ones[:, :], diagonal[:, tt, :],
                                            start=True, stop=True)
                last.then_inc(spread_ready, 1)

            def two_tiles(c, bank, turn=0, norm=None, middle=None):
                s = c % RING
                if c:
                    pe.wait_ge(split_done, RING * turn + c)
                order = [(t, k) for t in range(2) for k in range(KT)]
                if norm is not None:
                    order = [(t, k) for k in range(KT) for t in range(2)]
                for n, (t, k) in enumerate(order):
                    if norm is not None and t == 0:
                        pe.wait_ge(a_split, 8 * norm + k + 1)
                        if norm == 0 and k % 2 == 0:
                            pe.wait_ge(first_split, k // 2 + 1)
                    if norm and n == 14:
                        stats(norm)
                    if middle and n == 8:
                        middle()
                    for m, (w, part) in enumerate(passes(s, (2 * k + t) * P, P)):
                        first = m == 0 and (n == 0 if norm is not None else k == 0)
                        last = nc.tensor.matmul(bank[:, t, :], w, (a_hi if part == "hi" else a_lo)[:, k, :],
                                                start=first, stop=(m == 2 and k == KT - 1),
                                                skip_group_check=norm is not None)
                last.then_inc(chunk_used, 1)

            def project(c, b_hi, b_lo, first, last_one, turn=0):
                s = c % RING
                if c:
                    pe.wait_ge(split_done, RING * turn + c)
                for d in range(KT):
                    for k in range(2):
                        for m, (w, part) in enumerate(passes(s, (KT * k + d) * P, P)):
                            mm = nc.tensor.matmul(acc[d // 2][:, d % 2, :], w, (b_hi if part == "hi" else b_lo)[:, k, :],
                                                  start=(first and d % 2 == 0 and k == 0 and m == 0),
                                                  stop=(last_one and k == 1 and m == 2), skip_group_check=True)
                    if last_one and d in (1, 3, 5):
                        mm.then_inc(acc_ready, 1)
                mm.then_inc(chunk_used, 1)

            def gate_up_tile(f, jt, turn=0, norm=None, middle=None):
                t = f * FF_TILES + jt
                if jt >= 2:
                    pe.wait_ge(scaled, 2 * turn + t - 1)
                two_tiles(gate_chunk(f, jt), proj[jt % 2], turn, norm, middle)

            def down(f, pair, buf, turn=0):
                pe.wait_ge(h_split, turn + f * FF_PAIRS + pair + 1)
                project(down_chunk(f, pair), h_hi[:, buf], h_lo[:, buf], pair == 0, pair == FF_PAIRS - 1, turn)

            def ffn(f):
                n = nth_norm(FFN_NORM[f])
                gate_up_tile(f, 0, norm=FFN_NORM[f])
                gate_up_tile(f, 1, middle=(lambda: spread(n)) if f else (lambda: stats(0)))
                if f == 0:
                    spread(0)
                for j in (2, 3):
                    gate_up_tile(f, j)
                down(f, 0, 0)
                with pe.Fori(0, FF_PAIRS - 3) as i:
                    for j in (4, 5):
                        gate_up_tile(f, j, i)
                    down(f, 1, 0, i)
                last = FF_TILES - 2
                gate_up_tile(f, last)
                gate_up_tile(f, last + 1)
                down(f, FF_PAIRS - 2, 0)
                down(f, FF_PAIRS - 1, 1)

            def scores(hd):
                pe.wait_ge(rope_sum, 4 * hd + 4)
                if hd >= 2:
                    pe.wait_ge(decay_done, hd - 1)
                flat = misc[hd % 2][:, :, :].rearrange("p a t -> p (a t)")
                for key, (at, q0) in enumerate(((0, 0), (TOKENS, P))):
                    for t in range(2):
                        last = nc.tensor.matmul(flat[:, at:at + TOKENS - q0], qk[:, hd % 2, 1, t, key * P:(key + 1) * P],
                                                qk[:, hd % 2, 0, t, q0:TOKENS], start=(t == 0), stop=(t == 1))
                last.then_inc(scores_ready, 1)

            def head_values(hd):
                for half in range(2):
                    c = v_chunk(hd, half)
                    s = c % RING
                    pe.wait_ge(split_done, c)
                    if hd >= 2 and half == 0:
                        pe.wait_ge(v_kept, 2 * (hd - 1))
                    for tt in range(2):
                        for k in range(4):
                            w = slice(k * RET_V, (k + 1) * RET_V)
                            kk = 4 * half + k
                            tok = slice(tt * P, (tt + 1) * P)
                            for m, (a, b) in enumerate(((a_hi, w_hi), (a_lo, w_hi), (a_hi, w_lo))):
                                last = nc.tensor.matmul(acc[2 * (hd % 2) + tt][:, :, :].rearrange("p a t -> p (a t)"),
                                                        a[:, kk, tok], b[:, s, w],
                                                        start=(kk == 0 and m == 0), stop=(kk == 7 and m == 2),
                                                        skip_group_check=True)
                    last.then_inc(chunk_used, 1)

            def retained(hd):
                if hd == 0:
                    pe.wait_ge(decay_done, RET_HEADS)
                    pe.wait_ge(v_kept, 2 * RET_HEADS)
                elif hd == 1:
                    pe.wait_ge(o_kept, 2)
                else:
                    pe.wait_ge(y_done, 2 * hd)
                for t in range(V_TILES):
                    w = slice(hd * RET_V + t * P, hd * RET_V + (t + 1) * P)
                    nc.tensor.matmul(misc[t // 2][:, t % 2, :], values[:, 0, w], decayed[:, hd, 0:TOKENS],
                                     start=True, stop=False)
                    last = nc.tensor.matmul(misc[t // 2][:, t % 2, P:TOKENS], values[:, 1, w],
                                            decayed[:, hd, TOKENS:BAND], start=False, stop=True)
                last.then_inc(o_ready, 1)

            def mean_sum(hd):
                pe.wait_ge(o_added, 2 * hd + 1)
                for half in range(2):
                    last = nc.tensor.matmul(mean_bank(hd)[:, 0, :], ones[:, :], o_sum[:, half, :],
                                            start=(half == 0), stop=(half == 1))
                last.then_inc(mean_ready, 1)

            def square_sum(hd):
                pe.wait_ge(o_added, 2 * hd + 2)
                sums(nth_head(hd), [o_sum[:, half, :] for half in range(2)])

            def retention():
                for hd in range(RET_HEADS):
                    for which in range(2):
                        if hd:
                            pe.wait_ge(roped, 2 * (2 * (hd - 1) + which) + 2)
                        two_tiles((q_chunk, k_chunk)[which](hd), proj[which],
                                  norm=RET_NORM if hd == which == 0 else None,
                                  middle=(lambda: spread(nth_norm(RET_NORM))) if hd == 0 and which == 1 else None)
                    if hd:
                        scores(hd - 1)
                head_values(0)
                scores(RET_HEADS - 1)
                for hd in range(1, RET_HEADS):
                    head_values(hd)
                to_spread = None
                for kind, hd in RET_TAIL:
                    if kind == "g":
                        retained(hd)
                        if hd == 1:
                            spread(nth_head(0))
                            to_spread = None
                    for half in range(2):
                        c = tail_chunk(kind, hd, half)
                        if kind == "g":
                            if hd:
                                pe.wait_ge(g_scaled, 2 * (hd - 1) + half + 1)
                            else:
                                pe.wait_ge(rope_sum, 4 * RET_HEADS)
                            two_tiles(c, proj[half])
                        else:
                            pe.wait_ge(y_split, 2 * hd + half + 1)
                            if hd == half == 0:
                                pe.wait_ge(y_split, 2)
                            t = 4 * (hd % 2) + 2 * half
                            project(c, y_hi[:, t:t + 2, :], y_lo[:, t:t + 2, :],
                                    hd == half == 0, hd == RET_HEADS - 1 and half == 1)
                        if to_spread is not None:
                            spread(nth_head(to_spread))
                            to_spread = None
                        if kind == "g":
                            (mean_sum, square_sum)[half](hd)
                            if half == 1:
                                to_spread = hd

            def attention():
                n0 = ATT_AT
                two_tiles(n0, proj[0], norm=ATT_NORM)
                vm = nth_norm(ATT_NORM)
                s = (n0 + 1) % RING
                pe.wait_ge(split_done, n0 + 1)
                for tt in range(2):
                    if tt == 1:
                        spread(vm)
                    for k in range(KT):
                        for m, (a, b) in enumerate(((a_hi, w_hi), (a_lo, w_hi), (a_hi, w_lo))):
                            last = nc.tensor.matmul(proj[1][:, tt, :], a[:, k, tt * P:(tt + 1) * P],
                                                    b[:, s, k * 256:(k + 1) * 256],
                                                    start=(k == 0 and m == 0), stop=(k == 7 and m == 2))
                last.then_inc(chunk_used, 1)

                def q_tiles(c):
                    if c == 0:
                        pe.wait_ge(kqv_scaled, 1)
                    elif c == 1:
                        pe.wait_ge(v_done, 2)
                    else:
                        pe.wait_ge(kqv_scaled, c)
                    two_tiles(n0 + 2 + c, proj[c % 2])

                def query_scores(c):
                    pe.wait_ge(q_done, 2 * c + 2)
                    if c == 0:
                        pe.wait_ge(k_done, 2)
                        pe.wait_ge(rstd_done, ATT_NORM + 1)
                    elif c == 2:
                        pe.wait_ge(exp_done, 10)
                    elif c == 3:
                        pe.wait_ge(kqv_scaled, 5)
                    for f in range(2):
                        rows = slice(HEAD * f, HEAD * f + HEAD)
                        for t in range(2):
                            for n in range(4):
                                k0, width = (0, CHUNK) if n == 0 else (CHUNK * (n - 1), 2 * CHUNK)
                                to = (n // 2) * P
                                half = CHUNK * (n % 2)
                                last = nc.tensor.matmul(scores_bank(2 * c + f)[half:half + CHUNK, t, to:to + width],
                                                        att_q[rows, 2 * c + t, CHUNK * n:CHUNK * n + CHUNK],
                                                        att_k[rows, c // 2, k0:k0 + width], start=True, stop=True)
                        last.then_inc(att_scores, 1)

                def turn_probs(i):
                    pe.wait_ge(probs_done, i + 1)
                    if i == 0:
                        pe.wait_ge(ident_landed, 16)
                    if i >= 2:
                        pe.wait_ge(turned_kept, i - 1)
                    flat = turned_bank(i)[:, :, :].rearrange("p a t -> p (a t)")
                    for b in range(4):
                        last = nc.tensor.transpose(flat[:, b * P:(b + 1) * P], exps[i % 6][:, b, :],
                                                   consts[:, IDENT:IDENT + P])
                    last.then_inc(turned, 1)

                def mix(g):
                    pe.wait_ge(turned_kept, 4 * g + 4)
                    pe.wait_ge(v_shifted, 32)
                    for c in range(4):
                        bank = mix_bank(g, c // 2)
                        tok = (0, 0, 2, 1)[c]
                        for f in range(2):
                            kv = 2 * g + f
                            at = (2 * f + c // 2) * P + (c % 2) * CHUNK
                            last = nc.tensor.matmul(
                                bank[HEAD * f:HEAD * f + HEAD, :, CHUNK * (c % 2):CHUNK * (c % 2) + CHUNK],
                                att_v[:, tok, kv * HEAD:(kv + 1) * HEAD],
                                probs_t[:, 4 * g:4 * g + 4, at:at + CHUNK], start=True, stop=True)
                    last.then_inc(mixed, 1)

                def out_tiles(c):
                    pe.wait_ge(mixed_split, 2 * (c // 2) + 2)
                    project(n0 + 6 + c, y_hi[:, 2 * c:2 * c + 2, :], y_lo[:, 2 * c:2 * c + 2, :], c == 0, c == 3)

                q_tiles(0)
                q_tiles(1)
                query_scores(0)
                q_tiles(2)
                query_scores(1)
                turn_probs(0)
                turn_probs(1)
                q_tiles(3)
                query_scores(2)
                turn_probs(2)
                turn_probs(3)
                mix(0)
                query_scores(3)
                out_tiles(0)
                for u in range(4, 8):
                    turn_probs(u)
                mix(1)
                out_tiles(1)
                out_tiles(2)
                out_tiles(3)

            ffn(0)
            retention()
            ffn(1)
            ffn(2)
            attention()
            ffn(3)
            stats(LAST_NORM)
            spread(nth_norm(LAST_NORM))


def laid_out(inputs):
    a = {n: np.asarray(v) for n, v in inputs.items()}

    def columns(w):
        n = w.shape[1] // (2 * P)
        return w.reshape(KT, P, n, 2, P).transpose(2, 1, 0, 3, 4).reshape(n, P, WORDS)

    def rows(w):
        n = w.shape[0] // (2 * P)
        return w.reshape(n, 2, P, KT, P).transpose(0, 2, 1, 3, 4).reshape(n, P, WORDS)

    def ffn(w_in, w_out):
        gate, up = w_in[:, :D_FF].reshape(D_MODEL, FF_TILES, P), w_in[:, D_FF:].reshape(D_MODEL, FF_TILES, P)
        tiles = columns(np.stack([gate, up], 2).reshape(D_MODEL, 2 * D_FF))
        down = rows(w_out)
        order = [tiles[0], tiles[1]]
        for i in range(1, FF_PAIRS):
            order += [tiles[2 * i], tiles[2 * i + 1], down[i - 1]]
        return order + [down[FF_PAIRS - 1]]

    def ret(w_in, w_out):
        q, k, v, g = np.split(w_in, [D_MODEL, 2 * D_MODEL, 4 * D_MODEL], axis=1)
        q, k, g, o = columns(q), columns(k), columns(g), rows(w_out)
        order = []
        for hd in range(RET_HEADS):
            order += [q[hd], k[hd]]
        for hd in range(RET_HEADS):
            for half in range(2):
                part = v[half * 512:(half + 1) * 512, hd * RET_V:(hd + 1) * RET_V]
                order.append(part.reshape(4, P, RET_V).transpose(1, 0, 2).reshape(P, WORDS))
        for which, hd in ((g, 0), (g, 1), (o, 0), (g, 2), (o, 1), (g, 3), (o, 2), (o, 3)):
            order += [which[2 * hd], which[2 * hd + 1]]
        return order

    heads = [8 * (i // 4) + 4 * f + i % 4 for i in range(8) for f in range(2)]
    q_cols = np.concatenate([np.arange(HEAD) + HEAD * n for n in heads])

    def att(w_in, w_out):
        q, k, v = w_in[:, :1024][:, q_cols], w_in[:, 1024:1280], w_in[:, 1280:]
        v = v.reshape(KT, P, 256).transpose(1, 0, 2).reshape(P, WORDS)
        return [columns(k)[0], v, *columns(q), *rows(w_out[q_cols])]

    up1, down1, up2, down2 = (a[n] for n in ("ffn1_w_gate_up", "ffn1_w_down", "ffn2_w_gate_up", "ffn2_w_down"))
    weights = np.stack(ffn(up1[0], down1[0]) + ret(a["ret_w_in"][0], a["ret_w_out"][0]) + ffn(up2[0], down2[0])
                       + ffn(up1[1], down1[1]) + att(a["att_w_in"][0], a["att_w_out"][0]) + ffn(up2[1], down2[1]))

    def by_tile(v):
        return v.reshape(-1, P).T

    norms = [a["ffn1_norm"][0], a["mix_norm"][0], a["ffn2_norm"][0], a["ffn1_norm"][1], a["mix_norm"][1],
             a["ffn2_norm"][1], a["final_norm"]]
    b_in = a["att_b_in"][0]
    sinks = a["att_sinks"][0][np.array(heads)].reshape(4, 2, 2).transpose(0, 2, 1).reshape(-1).repeat(2)
    params = np.concatenate([*map(by_tile, norms), by_tile(a["ret_gn_gain"][0]), by_tile(b_in[:1024][q_cols]),
                             by_tile(b_in[1024:1280]), by_tile(a["att_b_out"][0]),
                             np.broadcast_to(sinks, (P, 32)), np.broadcast_to(b_in[1280:], (P, 256))], axis=1)
    x = a["x"][0].T.reshape(KT, P, TOKENS).transpose(1, 0, 2)
    return {"x_in": x, "weights": weights, "params_in": params, "consts_in": constants()}


def constants():
    f = np.float32
    theta = f(10000.0) ** (-np.linspace(0.0, 1.0, RET_QK // 2, dtype=f))
    angle = np.arange(TOKENS, dtype=f)[None, :] * theta[:, None]
    log_gamma = np.log(1.0 - 2.0 ** (-5.0 - np.arange(RET_HEADS)))
    key, query = np.arange(TOKENS)[:, None], np.arange(TOKENS)[None, :]
    decay = np.exp(log_gamma[:, None, None] * np.abs(query - key)) * (query // CHUNK >= key // CHUNK)
    decay = decay * RET_QK ** -0.5
    band = [np.concatenate([d[:P], d[P:, P:]], axis=1) for d in decay]
    return np.concatenate([np.cos(angle), np.sin(angle), np.eye(P), *band], axis=1).astype(f)


def kernel(**inputs):
    import concourse.bacc as bacc
    from concourse.bass_utils import run_bass_kernel_spmd

    nc = bacc.Bacc("TRN2", target_bir_lowering=False, num_devices=1)
    arrays, args = {}, []
    for name, v in laid_out(inputs).items():
        v = np.ascontiguousarray(v)
        arrays[name] = v
        args.append(nc.dram_tensor(name, v.shape, mybir.dt.from_np(v.dtype), kind="ExternalInput").ap())
    out = nc.dram_tensor("out", (P, KT, TOKENS), F32, kind="ExternalOutput").ap()
    trunk(nc, *args, out)
    r = run_bass_kernel_spmd(nc, [arrays], core_ids=[0])
    got = np.asarray(r.results[0]["out"])
    return np.ascontiguousarray(got.transpose(2, 1, 0).reshape(1, TOKENS, D_MODEL))
```
